# Optimizing a Trainium2 kernel written in Bass

```python
import jax, jax.numpy as jnp
from jax import lax
import numpy as np

D_MODEL = 1024
BATCH = 1
SEQ = 512
DEPTH = 1
DEC_BATCH = 1
DEC_SEQ = 64
PAST_LEN = 512

CHUNK = 64
D_PLE = 256
D_CONV = 512
CONV_WIDTH = 31
CONV_STATE = CONV_WIDTH - 1
N_HEADS = 8
N_KV_HEADS = 2
HEAD_DIM = 64
GROUP = N_HEADS // N_KV_HEADS
WINDOW = 128
BAND = WINDOW + CHUNK
D_ATTN = N_HEADS * HEAD_DIM
D_KV = N_KV_HEADS * HEAD_DIM
OFF_Q = 2 * D_CONV
OFF_K = OFF_Q + D_ATTN
OFF_V = OFF_K + D_KV
OFF_GATE = OFF_V + D_KV
D_IN = OFF_GATE + 2 * D_MODEL
N_KEYS = 128
N_EXPERTS = N_KEYS * N_KEYS
N_RET_HEADS = 8
D_QUERY = 256
D_HALF = D_QUERY // 2
TOPK_HALF = 16
TOPK = 16
PEER_BLOCK = 128
EPS = 1e-6
NEG_INF = -1e30

kernel_name = 'gated_conformer_swa_peer_stream'

def rms_norm(x, g):
    x32 = x.astype(jnp.float32)
    y = x32 * lax.rsqrt(jnp.mean(x32 * x32, axis=-1, keepdims=True) + EPS)
    return (y * g.astype(jnp.float32)).astype(x.dtype)

def layer_norm(x, g, b):
    x32 = x.astype(jnp.float32)
    mu = jnp.mean(x32, axis=-1, keepdims=True)
    var = jnp.mean(jnp.square(x32 - mu), axis=-1, keepdims=True)
    y = (x32 - mu) * lax.rsqrt(var + EPS) * g.astype(jnp.float32) + b.astype(jnp.float32)
    return y.astype(x.dtype)

def alibi_slopes():
    return jnp.asarray(2.0 ** (-8.0 * np.arange(1, N_HEADS + 1) / N_HEADS), dtype=jnp.float32)

def attend_band(q, k, v, offset, valid, sinks):
    nq, nk = q.shape[-4], k.shape[-3]
    s = jnp.einsum('...qkgd,...skd->...kgqs', q, k,
                   preferred_element_type=jnp.float32) * (HEAD_DIM ** -0.5)
    dist = jnp.abs(jnp.arange(nq)[:, None] + offset - jnp.arange(nk)[None, :]).astype(jnp.float32)
    slopes = alibi_slopes().reshape(N_KV_HEADS, GROUP)
    s = s - slopes[:, :, None, None] * dist
    if valid is not None:
        s = jnp.where(valid[..., None, None, None, :], s, NEG_INF)
    sink = sinks.astype(jnp.float32).reshape(N_KV_HEADS, GROUP)[:, :, None, None]
    lse = jnp.logaddexp(jax.nn.logsumexp(s, axis=-1, keepdims=True), sink)
    p = jnp.exp(s - lse).astype(v.dtype)
    return jnp.einsum('...kgqs,...skd->...qkgd', p, v)

def attn_prompt(q, k, v, sinks):
    B, S = q.shape[0], q.shape[1]
    n_chunks = S // CHUNK
    qb = q.reshape(B, n_chunks, CHUNK, N_KV_HEADS, GROUP, HEAD_DIM)
    kp = jnp.pad(k, ((0, 0), (WINDOW, 0), (0, 0), (0, 0)))
    vp = jnp.pad(v, ((0, 0), (WINDOW, 0), (0, 0), (0, 0)))
    idx = jnp.arange(n_chunks)[:, None] * CHUNK + jnp.arange(BAND)[None, :]
    kb = kp[:, idx]
    vb = vp[:, idx]
    valid = idx >= WINDOW
    o = attend_band(qb, kb, vb, WINDOW, valid, sinks)
    return o.reshape(B, S, D_ATTN)

def attn_sample(q, k, v, past_k, past_v, sinks):
    B, T = q.shape[0], q.shape[1]
    kk = jnp.concatenate([past_k, k], axis=1)
    vv = jnp.concatenate([past_v, v], axis=1)
    qb = q.reshape(B, T, N_KV_HEADS, GROUP, HEAD_DIM)
    o = attend_band(qb, kk, vv, past_k.shape[1], None, sinks)
    return o.reshape(B, T, D_ATTN)

def depthwise_causal(xp, w, b):
    y = lax.conv_general_dilated(xp, w[:, None, :], window_strides=(1,), padding='VALID',
                                 dimension_numbers=('NWC', 'WIO', 'NWC'),
                                 feature_group_count=D_CONV)
    return y + b

def peer(h, w_query, sub_keys1, sub_keys2, expert_u, expert_v):
    T = h.shape[0]
    nb = -(-T // PEER_BLOCK)
    hp = jnp.pad(h, ((0, nb * PEER_BLOCK - T), (0, 0))).reshape(nb, PEER_BLOCK, D_MODEL)

    def block(hb):
        q = (hb @ w_query).reshape(PEER_BLOCK, N_RET_HEADS, D_QUERY)
        s1 = jnp.einsum('trd,nd->trn', q[..., :D_HALF], sub_keys1, preferred_element_type=jnp.float32)
        s2 = jnp.einsum('trd,nd->trn', q[..., D_HALF:], sub_keys2, preferred_element_type=jnp.float32)
        v1, i1 = lax.top_k(s1, TOPK_HALF)
        v2, i2 = lax.top_k(s2, TOPK_HALF)
        cand = (v1[..., :, None] + v2[..., None, :]).reshape(PEER_BLOCK, N_RET_HEADS, TOPK_HALF * TOPK_HALF)
        cidx = (i1[..., :, None] * N_KEYS + i2[..., None, :]).reshape(PEER_BLOCK, N_RET_HEADS, TOPK_HALF * TOPK_HALF)
        sv, si = lax.top_k(cand, TOPK)
        eidx = jnp.take_along_axis(cidx, si, axis=-1)
        g = jax.nn.softmax(sv, axis=-1)
        ue = jnp.take(expert_u, eidx, axis=0)
        a = jnp.einsum('trkd,td->trk', ue, hb, preferred_element_type=jnp.float32)
        act = (jax.nn.gelu(a) * g).astype(hb.dtype)
        ve = jnp.take(expert_v, eidx, axis=0)
        return jnp.einsum('trk,trkd->td', act, ve)

    out = lax.map(block, hp).reshape(nb * PEER_BLOCK, D_MODEL)
    return out[:T]

def trunk_layer(x, p, past_k, past_v, past_conv,
                g_mix, w_in, b_in, w_dw, b_dw, g_cln, b_cln, w_cout, b_cout, sinks, w_aout, w_out,
                g_ffn, w_query, sub_keys1, sub_keys2, expert_u, expert_v, w_ple, g_ple, w_ple_gate):
    B, T, _ = x.shape
    h = rms_norm(x, g_mix)
    z = h @ w_in + b_in
    glu = z[..., :D_CONV] * jax.nn.sigmoid(z[..., D_CONV:OFF_Q])
    q = z[..., OFF_Q:OFF_K].reshape(B, T, N_HEADS, HEAD_DIM)
    k = z[..., OFF_K:OFF_V].reshape(B, T, N_KV_HEADS, HEAD_DIM)
    v = z[..., OFF_V:OFF_GATE].reshape(B, T, N_KV_HEADS, HEAD_DIM)
    gates = jax.nn.sigmoid(z[..., OFF_GATE:])
    if past_conv is None:
        conv_in = jnp.pad(glu, ((0, 0), (CONV_STATE, 0), (0, 0)))
        att = attn_prompt(q, k, v, sinks)
        new_k = k[:, -WINDOW:]
        new_v = v[:, -WINDOW:]
    else:
        conv_in = jnp.concatenate([past_conv, glu], axis=1)
        att = attn_sample(q, k, v, past_k, past_v, sinks)
        n_keep = past_k.shape[1]
        new_k = jnp.concatenate([past_k, k], axis=1)[:, -n_keep:]
        new_v = jnp.concatenate([past_v, v], axis=1)[:, -n_keep:]
    new_conv = conv_in[:, -CONV_STATE:]
    c = jax.nn.silu(layer_norm(depthwise_causal(conv_in, w_dw, b_dw), g_cln, b_cln))
    branch_a = c @ w_cout + b_cout
    branch_b = att @ w_aout
    merged = gates[..., :D_MODEL] * branch_a + gates[..., D_MODEL:] * branch_b
    x = x + merged @ w_out
    h2 = rms_norm(x, g_ffn)
    x = x + peer(h2.reshape(B * T, D_MODEL), w_query, sub_keys1, sub_keys2,
                 expert_u, expert_v).reshape(B, T, D_MODEL)
    ple_gate = jax.nn.sigmoid(rms_norm(x, g_ple) @ w_ple_gate)
    x = x + ple_gate * (p @ w_ple)
    return x, new_k, new_v, new_conv

def setup_inputs(seed: int = 0) -> dict:
    key = jax.random.key(seed)
    ks = jax.random.split(key, 32)
    f32 = jnp.float32

    def nrm(k, shape, scale):
        return jax.random.normal(k, shape, f32) * scale

    def gain(k, shape):
        return 1.0 + 0.1 * jax.random.normal(k, shape, f32)

    kv_cache = min(WINDOW, PAST_LEN)
    return {
        'x_prompt': nrm(ks[0], (BATCH, SEQ, D_MODEL), 1.0),
        'x_sample': nrm(ks[1], (DEC_BATCH, DEC_SEQ, D_MODEL), 1.0),
        'p_prompt': nrm(ks[2], (DEPTH, BATCH, SEQ, D_PLE), 1.0),
        'p_sample': nrm(ks[3], (DEPTH, DEC_BATCH, DEC_SEQ, D_PLE), 1.0),
        'cache_k': nrm(ks[4], (DEPTH, DEC_BATCH, kv_cache, N_KV_HEADS, HEAD_DIM), 1.0),
        'cache_v': nrm(ks[5], (DEPTH, DEC_BATCH, kv_cache, N_KV_HEADS, HEAD_DIM), 1.0),
        'state_conv': nrm(ks[6], (DEPTH, DEC_BATCH, CONV_STATE, D_CONV), 0.5),
        'g_mix': gain(ks[7], (DEPTH, D_MODEL)),
        'w_in': nrm(ks[8], (DEPTH, D_MODEL, D_IN), D_MODEL ** -0.5),
        'b_in': nrm(ks[9], (DEPTH, D_IN), 0.02),
        'w_dw': nrm(ks[10], (DEPTH, CONV_WIDTH, D_CONV), CONV_WIDTH ** -0.5),
        'b_dw': nrm(ks[11], (DEPTH, D_CONV), 0.02),
        'g_cln': gain(ks[12], (DEPTH, D_CONV)),
        'b_cln': nrm(ks[13], (DEPTH, D_CONV), 0.02),
        'w_cout': nrm(ks[14], (DEPTH, D_CONV, D_MODEL), D_CONV ** -0.5),
        'b_cout': nrm(ks[15], (DEPTH, D_MODEL), 0.02),
        'sinks': nrm(ks[16], (DEPTH, N_HEADS), 1.0),
        'w_aout': nrm(ks[17], (DEPTH, D_ATTN, D_MODEL), D_ATTN ** -0.5),
        'w_out': nrm(ks[18], (DEPTH, D_MODEL, D_MODEL), D_MODEL ** -0.5),
        'g_ffn': gain(ks[19], (DEPTH, D_MODEL)),
        'w_query': nrm(ks[20], (DEPTH, D_MODEL, N_RET_HEADS * D_QUERY), D_MODEL ** -0.5),
        'sub_keys1': nrm(ks[21], (DEPTH, N_KEYS, D_HALF), D_HALF ** -0.5),
        'sub_keys2': nrm(ks[22], (DEPTH, N_KEYS, D_HALF), D_HALF ** -0.5),
        'expert_u': nrm(ks[23], (DEPTH, N_EXPERTS, D_MODEL), D_MODEL ** -0.5),
        'expert_v': nrm(ks[24], (DEPTH, N_EXPERTS, D_MODEL), 0.5),
        'w_ple': nrm(ks[25], (DEPTH, D_PLE, D_MODEL), D_PLE ** -0.5),
        'g_ple': gain(ks[26], (DEPTH, D_MODEL)),
        'w_ple_gate': nrm(ks[27], (DEPTH, D_MODEL, D_MODEL), D_MODEL ** -0.5),
        'g_final': gain(ks[28], (D_MODEL,)),
    }

def reference(x_prompt, x_sample, p_prompt, p_sample, cache_k, cache_v, state_conv,
              g_mix, w_in, b_in, w_dw, b_dw, g_cln, b_cln, w_cout, b_cout, sinks, w_aout, w_out,
              g_ffn, w_query, sub_keys1, sub_keys2, expert_u, expert_v, w_ple, g_ple, w_ple_gate,
              g_final):
    xp, xs = x_prompt, x_sample
    kp_l, vp_l, cp_l, ks_l, vs_l, cs_l = [], [], [], [], [], []
    for i in range(DEPTH):
        w = (g_mix[i], w_in[i], b_in[i], w_dw[i], b_dw[i], g_cln[i], b_cln[i], w_cout[i], b_cout[i],
             sinks[i], w_aout[i], w_out[i], g_ffn[i], w_query[i], sub_keys1[i], sub_keys2[i],
             expert_u[i], expert_v[i], w_ple[i], g_ple[i], w_ple_gate[i])
        xp, nk, nv, nc = trunk_layer(xp, p_prompt[i], None, None, None, *w)
        kp_l.append(nk); vp_l.append(nv); cp_l.append(nc)
        xs, nk, nv, nc = trunk_layer(xs, p_sample[i], cache_k[i], cache_v[i], state_conv[i], *w)
        ks_l.append(nk); vs_l.append(nv); cs_l.append(nc)
    y_prompt = rms_norm(xp, g_final)
    y_sample = rms_norm(xs, g_final)
    return (y_prompt, y_sample,
            jnp.stack(kp_l), jnp.stack(vp_l), jnp.stack(cp_l),
            jnp.stack(ks_l), jnp.stack(vs_l), jnp.stack(cs_l))


_drawn_inputs = setup_inputs


def setup_inputs(seed=0):
    import zlib

    import numpy as np

    out = dict(_drawn_inputs(seed))
    spreads = {}
    factors = {'b_cln': 2.878, 'g_ple': 3.145}
    for name, (base, spread) in spreads.items():
        noise = np.random.default_rng([zlib.crc32(name.encode()), seed]).standard_normal(out[name].shape)
        drawn = base * np.exp(spread * noise) if base else spread * noise
        out[name] = __import__('jax').numpy.asarray(drawn.astype(out[name].dtype))
    for name, factor in factors.items():
        out[name] = (out[name] * factor).astype(out[name].dtype)
    return out
```

```python
from contextlib import ExitStack

import numpy as np

import concourse.bass as bass
from concourse import mybir

F32 = mybir.dt.float32
U32 = mybir.dt.uint32
ALU = mybir.AluOpType
ACT = mybir.ActivationFunctionType
AX = mybir.AxisListType.X

P = 128
D, DC, DP = 1024, 512, 256
KD, KC, KP = D // P, DC // P, DP // P
SEQ, DEC = 512, 64
TOK = SEQ + DEC
H, KV, HD = 8, 2, 64
PAIRS = H // KV
CHUNK, WINDOW = 64, 128
TAPS = 31
STATE = TAPS - 1
NZ = (2 * DC + H * HD + 2 * KV * HD + 2 * D) // P
HEADS, TOPK, KEYS = 8, 16, 128
SEGS = 2 * HEADS
PICKS = HEADS * TOPK
EPS = 1e-6
SLOPES = [2.0 ** (-8.0 * (h + 1) / H) for h in range(H)]
GELU_C, GELU_K = 0.044715, 0.7978845608028654
LOWEST = -3.0e38

TILES = [(0, 0, P), (0, P, P), (1, 0, P), (1, P, P), (1, 2 * P, DEC)]
GROUPS = [[t for t in range(len(TILES)) if TILES[t][0] == g] for g in range(2)]
WIDTH = [sum(TILES[t][2] for t in GROUPS[g]) for g in range(2)]
WMAX = max(WIDTH)
START = [0, WIDTH[0]]
SAMPLE = len(TILES) - 1
Q0, K0, V0, G0 = 2 * KC, 2 * KC + 4, 2 * KC + 5, 2 * KC + 6
ZORDER = [n for c in range(KC) for n in (KC + c, c)] + [K0, V0] + list(range(Q0, K0)) + list(range(G0, NZ))
SCALAR_Z = [n for n in ZORDER if n >= KC]
SEG = [[(0, 2 * P, STATE)], [(0, 2 * P, STATE), (2 * P, DEC, 2 * STATE + 2 * P)]]
CONVW = [2 * P, 2 * P + STATE + DEC]
GLUW = 2 * STATE + 2 * P + DEC
KCOLS = WINDOW + SEQ + WINDOW + DEC

BANKS = 4
WSLOTS = 6
SLOTS = 8
HALF = 8
ITERS = PICKS // (2 * HALF)
C_BIN, C_GMIX, C_BDW, C_GCLN, C_BCLN, C_BCOUT, C_WDW = 0, 30, 38, 42, 46, 50, 58
NCOLS = C_WDW + KC * TAPS


def plan_units():
    units, count = [], {}

    def unit(name, key, sem, step=1):
        count[sem] = count.get(sem, 0) + step
        units.append((name, key, sem, count[sem]))

    for g in range(2):
        unit("ms", g, "rms_x")
        for n in ZORDER:
            unit("z", (g, n), "scalar_z" if n >= KC else "glu")
        for t in GROUPS[g]:
            unit("vtok", t, "tokens_v")
        for t in GROUPS[g]:
            for j in range(PAIRS):
                unit("score", (t, j), "scores")
            for j in range(PAIRS):
                unit("probT", (t, j), "probs_t")
            unit("attT", t, "att_t")
        unit("mean", g, "centred")
        unit("var", g, "rms_conv")
        for n in range(KD):
            unit("conv_out", (g, n), "merged", 1)
            unit("attn_out", (g, n), "merged", 0)
        for n in range(KD):
            unit("mix", (g, n), "delta_t")
        for t in GROUPS[g]:
            for hf in range(2):
                unit("x1", (t, hf), "x1_ready")
            for hf in range(2):
                unit("h2T", (t, hf), "h2_t")
        for n in range(SEGS):
            unit("query", (g, n), "query_t")
        for t in GROUPS[g]:
            for j in range(4):
                unit("keyscore", (t, j), "key_scores")
        if g == 1:
            for s in range(2):
                unit("state", s, "conv_state")
    for t in range(len(TILES)):
        for hf in range(2):
            unit("h3T", (t, hf), "h3_t")
        for hf in range(2):
            unit("ple_gate", (t, hf), "ple_gate")
            unit("ple", (t, hf), "x3_half")
    return units


UNITS = plan_units()
AT = {(name, key): u for u, (name, key, _, _) in enumerate(UNITS)}
WEIGHTS = [
    (what, n, AT[unit, (g, n)])
    for g in range(2)
    for what, unit, order in (("w_in", "z", ZORDER), ("w_br", "attn_out", range(KD)),
                              ("w_out", "mix", range(KD)), ("w_query", "query", range(SEGS)))
    for n in order
]


def build(nc, a):
    ctx = ExitStack()

    def sb(name, shape, dt=F32, stack=None):
        return (stack or ctx).enter_context(nc.sbuf_tensor(f"{name}_buf", shape, dt))

    with ctx:
        cols = sb("cols", [P, NCOLS])
        gains = sb("gains", [P, 3, D])
        ident = sb("ident_sb", [P, P])
        sinks = sb("sinks_sb", [P, H])
        dist = sb("dist_sb", [P, 2 * P])
        iota = sb("iota_sb", [P, TOPK])
        keys_t = sb("keys_t", [P, 2, KEYS])
        over_d = sb("over_d", [P, P])
        over_c = sb("over_c", [P, P])
        zeros = sb("zeros", [P, P])
        eps = sb("eps", [P, 1])
        w_ple = sb("w_ple_sb", [P, KP, D])
        p_t = sb("p_t_sb", [P, KP, TOK])
        x1 = sb("x1", [P, len(TILES), D])
        h2 = sb("h2", [P, len(TILES), D])
        expert = sb("expert", [P, len(TILES) * PICKS], U32)
        gate = sb("gate", [P, len(TILES) * PICKS])
        small = sb("small", [P, 64])
        dot = sb("dot", [P, PICKS])

        ring = [ctx.enter_context(nc.psum_tensor(f"ring{b}", [P, 512], F32)) for b in range(BANKS)]
        acc = ctx.enter_context(nc.psum_tensor("acc", [P, D], F32))

        sems = {}

        def sem(name):
            if name not in sems:
                sems[name] = ctx.enter_context(nc.semaphore(name))
            return sems[name]

        filled = sem("filled")
        loaded = {k: sem(f"loaded_{k}") for k in ("const", "xT0", "xT1", "x", "tail", "cache")}
        w_loaded = [sem(f"w_loaded{i}") for i in range(WSLOTS)]
        u_loaded = [sem(f"u_loaded{i}") for i in range(SLOTS)]
        v_loaded = [sem(f"v_loaded{i}") for i in range(SLOTS)]
        u_free, v_free = sem("u_free"), sem("v_free")
        stored = sem("stored")

        trunk = ExitStack()
        wring = sb("wring", [P, WSLOTS, KD, P], stack=trunk)
        hT = sb("hT", [P, KD, WMAX], stack=trunk)
        merged = sb("merged", [P, KD, WMAX], stack=trunk)
        gates = sb("gates", [P, SEGS, WMAX], stack=trunk)
        sig = sb("sig", [P, KC, WMAX], stack=trunk)
        qT = sb("qT", [P, PAIRS, WMAX], stack=trunk)
        kT = sb("kT", [P, KCOLS], stack=trunk)
        vT = sb("vT", [P, WMAX], stack=trunk)
        tmp = sb("tmp", [P, WMAX], stack=trunk)
        rstd = sb("rstd", [P, GLUW], stack=trunk)
        vtok = sb("vtok", [P, 6, P], stack=trunk)
        ktok = sb("ktok", [P, 2, P], stack=trunk)
        glu = sb("glu", [P, KC, GLUW], stack=trunk)
        conv = sb("conv", [P, KC, CONVW[1]], stack=trunk)
        convsq = merged[:].rearrange("p c n -> p (c n)")[:, 0:KC * CONVW[1]].rearrange("p (c n) -> p c n", c=KC)
        cT = sig
        past = sb("past", [P, KC, STATE], stack=trunk)
        stash = sb("stash", [STATE, 2, DC], stack=trunk)
        S = sb("S", [P, H, 2 * P], stack=trunk)
        PT = sb("PT", [P, H * 2, P], stack=trunk)
        attT = sb("attT", [P, PAIRS, WMAX], stack=trunk)
        best = sb("best", [P, SEGS, TOPK], stack=trunk)
        bestid = sb("bestid", [P, SEGS, TOPK], U32, stack=trunk)
        bestidf = sb("bestidf", [P, SEGS, TOPK], stack=trunk)
        top = sb("top", [P, HEADS, TOPK], stack=trunk)
        pos = sb("pos", [P, 3, HEADS, TOPK], U32, stack=trunk)
        posf = sb("posf", [P, 2, HEADS, TOPK], stack=trunk)
        chosen = sb("chosen", [P, 2, PICKS], stack=trunk)
        trunk.close()
        peer = ExitStack()
        uring = sb("uring", [P, SLOTS, D], stack=peer)
        vring = sb("vring", [P, SLOTS, D], stack=peer)
        w_pg = sb("w_pg_sb", [P, KD, D], stack=peer)
        diag = sb("diag", [P, 2, HALF, P], stack=peer)
        ids = sb("ids", [P, 4, HALF], U32, stack=peer)
        astage = sb("astage", [P, HALF], stack=peer)
        act = sb("act_sb", [P, 2 * PICKS], stack=peer)
        x2 = sb("x2", [P, D], stack=peer)
        h3 = sb("h3", [P, D], stack=peer)
        h3T = sb("h3T", [P, KD, P], stack=peer)
        pgate = sb("pgate", [P, D], stack=peer)
        y = sb("y", [P, 2, D], stack=peer)
        peer.close()

        block = ctx.enter_context(nc.Block())

        def bank(name, key):
            return ring[AT[name, key] % BANKS]

        def full(eng, name, key):
            eng.wait_ge(filled, AT[name, key] + 1)

        class Chain:

            def __init__(self, eng, own):
                self.eng, self.own, self.count = eng, own, {}

            def step(self, ins, name=None):
                s = sem(name) if name else self.own
                self.count[s] = self.count.get(s, 0) + 1
                ins.then_inc(s, 1)
                self.eng.wait_ge(s, self.count[s])

        @block.sync
        def _(sp):
            sp.dma_start(hT[:, :, 0:WIDTH[0]], a["x_t"][:, :, 0:WIDTH[0]]).then_inc(loaded["xT0"], 16)
            for name, to in (("cols", cols), ("ident", ident), ("dist", dist), ("iota", iota), ("keys_t", keys_t)):
                sp.dma_start(to[:], a[name]).then_inc(loaded["const"], 16)
            sp.dma_start(sinks[:], a["sinks"].to_broadcast([P, H])).then_inc(loaded["const"], 16)
            for i, name in enumerate(("g_ffn", "g_ple", "g_final")):
                sp.dma_start(gains[:, i, :], a[name].to_broadcast([P, D])).then_inc(loaded["const"], 16)
            sp.dma_start(kT[:, WINDOW + SEQ:2 * WINDOW + SEQ], a["cache_kt"]).then_inc(loaded["cache"], 16)
            sp.dma_start(vtok[:, 4, :], a["cache_v"]).then_inc(loaded["cache"], 16)
            sp.dma_start(past[:], a["past_t"]).then_inc(loaded["cache"], 16)

            def extra(i):
                if i == 8:
                    sp.dma_start(x1[:, 0:4, :], a["x_p"].rearrange("(t p) d -> p t d", p=P)).then_inc(loaded["x"], 16)
                    sp.dma_start(x1[0:DEC, 4, :], a["x_s"]).then_inc(loaded["x"], 16)
                    sp.dma_start(w_ple[:], a["w_ple"]).then_inc(loaded["tail"], 16)
                    sp.dma_start(p_t[:], a["p_t"]).then_inc(loaded["tail"], 16)
                    sp.dma_start(a["nk_s"][0:DEC, :], a["cache_k"][DEC:WINDOW, :]).then_inc(stored, 16)
                    sp.dma_start(a["nv_s"][0:DEC, :], a["cache_v"][DEC:WINDOW, :]).then_inc(stored, 16)
                if i == len(WEIGHTS) // 2:
                    full(sp, "x1", (GROUPS[0][-1], 1))
                    sp.dma_start(hT[:, :, 0:WIDTH[1]], a["x_t"][:, :, WIDTH[0]:TOK]).then_inc(loaded["xT1"], 16)

            for i, (what, n, _) in enumerate(WEIGHTS):
                extra(i)
                if i >= WSLOTS:
                    sp.wait_ge(filled, WEIGHTS[i - WSLOTS][2] + 1)
                sp.dma_start(wring[:, i % WSLOTS], a[what][n]).then_inc(w_loaded[i % WSLOTS], 16)
            sp.wait_ge(sem("tokens_v"), 5)
            for t, rows, nk, nv, at in ((3, P, "nk_p", "nv_p", 0), (4, DEC, "nk_s", "nv_s", DEC)):
                sp.dma_start(a[nk][at:at + rows, :], ktok[0:rows, t - 3, :]).then_inc(stored, 16)
                sp.dma_start(a[nv][at:at + rows, :], vtok[0:rows, 3 if t == 3 else 5, :]).then_inc(stored, 16)
            sp.wait_ge(sem("conv_state"), 2)
            for s, name in enumerate(("nc_p", "nc_s")):
                sp.dma_start(a[name], stash[:, s, :]).then_inc(stored, 16)
            sp.wait_ge(stored, 16 * 8)
            sp.wait_ge(sem("experts"), len(TILES))
            sp.dma_start(w_pg[:], a["w_pg"]).then_inc(loaded["tail"], 16)
            for t, (g, at, rows) in enumerate(TILES):
                sp.wait_ge(sem("y_ready"), t + 1)
                to = a["y_p"][t * P:(t + 1) * P, :] if t < 4 else a["y_s"]
                sp.dma_start(to, y[0:rows, t % 2, :]).then_inc(sem(f"y_stored{t % 2}"), 16)
            sp.wait_ge(sem("y_stored0"), 16 * 3)
            sp.wait_ge(sem("y_stored1"), 16 * 2)

        @block.tensor
        def _(pe):
            wi = [0]

            def begin(name, key):
                u = AT[name, key]
                if u >= BANKS:
                    pe.wait_ge(sem(UNITS[u - BANKS][2]), UNITS[u - BANKS][3])
                return ring[u % BANKS]

            def weights():
                i = wi[0]
                wi[0] += 1
                pe.wait_ge(w_loaded[i % WSLOTS], 16 * (i // WSLOTS + 1))
                return wring[:, i % WSLOTS]

            def product(out, w, x, ks, last=None):
                for c in range(ks):
                    ins = pe.matmul(out, w(c), x(c), start=(c == 0), stop=(c == ks - 1))
                return ins

            pe.wait_ge(loaded["const"], 16 * 9)
            pe.wait_ge(loaded["cache"], 16 * 3)
            pe.wait_ge(sem("filled_const"), 4)
            for g in range(2):
                n_tok, tiles, cw = WIDTH[g], GROUPS[g], CONVW[g]
                pe.wait_ge(sem("x_squared"), g + 1)
                out = begin("ms", g)
                product(out[:, 0:n_tok], lambda c: over_d[:], lambda c: merged[:, c, 0:n_tok], KD).then_inc(filled, 1)
                pe.wait_ge(sem("h_ready"), g + 1)
                for n in ZORDER:
                    out, w = begin("z", (g, n)), weights()
                    product(out[:, 0:n_tok], lambda c: w[:, c, :], lambda c: hT[:, c, 0:n_tok], KD).then_inc(filled, 1)
                zdone = len(SCALAR_Z) * g
                pe.wait_ge(sem("scalar_z"), zdone + SCALAR_Z.index(V0) + 1)
                for t in tiles:
                    _, at, rows = TILES[t]
                    kat = WINDOW + t * P if t < SAMPLE else KCOLS - DEC
                    out = begin("vtok", t)
                    pe.transpose(out[0:rows, 0:P], vT[:, at:at + rows], ident[:])
                    pe.transpose(out[0:rows, P:2 * P], kT[:, kat:kat + rows], ident[:]).then_inc(filled, 1)
                for t in tiles:
                    _, at, rows = TILES[t]
                    lo, hi = (P if t == 0 else 0), (2 * P if t < SAMPLE else WINDOW + DEC)
                    band = t * P if t < SAMPLE else WINDOW + SEQ
                    pe.wait_ge(sem("scalar_z"), zdone + SCALAR_Z.index(K0 - 1) + 1)
                    for j in range(PAIRS):
                        out = begin("score", (t, j))
                        f = slice(j // 2 * HD, (j // 2 + 1) * HD)
                        for b in range(2):
                            ins = pe.matmul(out[0:rows, b * 2 * P + lo:b * 2 * P + hi], qT[f, j % 2 * 2 + b, at:at + rows],
                                            kT[f, band + lo:band + hi], start=True, stop=True)
                        ins.then_inc(filled, 1)
                    pe.wait_ge(sem("probs"), t + 1)
                    for j in range(PAIRS):
                        out = begin("probT", (t, j))
                        for kv in range(KV):
                            for part in range(lo // P, 2):
                                a0, a1 = part * P, min((part + 1) * P, hi)
                                b = (2 * kv + part) * P
                                ins = pe.transpose(out[0:a1 - a0, b:b + rows], S[0:rows, PAIRS * kv + j, a0:a1],
                                                   ident[0:rows, 0:rows])
                        ins.then_inc(filled, 1)
                    pe.wait_ge(sem("probs_t"), PAIRS * (t + 1))
                    pe.wait_ge(sem("tokens_v"), t + 1)
                    out = begin("attT", t)
                    for j in range(PAIRS):
                        for kv in range(KV):
                            for part in range(lo // P, 2):
                                n_k = min((part + 1) * P, hi) - part * P
                                vt = t - 1 + part if t < SAMPLE else 4 + part
                                ins = pe.matmul(out[kv * HD:(kv + 1) * HD, j * P:j * P + rows],
                                                vtok[0:n_k, vt, kv * HD:(kv + 1) * HD],
                                                PT[0:n_k, 4 * j + 2 * kv + part, 0:rows],
                                                start=(part == lo // P), stop=(part == 1))
                    ins.then_inc(filled, 1)
                pe.wait_ge(sem("conv"), KC * TAPS * (g + 1))
                out = begin("mean", g)
                product(out[:, 0:cw], lambda c: over_c[:], lambda c: conv[:, c, 0:cw], KC).then_inc(filled, 1)
                pe.wait_ge(sem("conv_squared"), g + 1)
                out = begin("var", g)
                product(out[:, 0:cw], lambda c: over_c[:], lambda c: convsq[:, c, 0:cw], KC).then_inc(filled, 1)
                pe.wait_ge(sem("silu"), g + 1)
                pe.wait_ge(sem("att_t"), tiles[-1] + 1)
                for n in range(KD):
                    out, w = begin("conv_out", (g, n)), weights()
                    product(out[:, 0:n_tok], lambda c: w[:, c, :], lambda c: cT[:, c, 0:n_tok], KC).then_inc(filled, 1)
                    out = begin("attn_out", (g, n))
                    product(out[:, 0:n_tok], lambda c: w[:, KC + c, :], lambda c: attT[:, c, 0:n_tok], KC).then_inc(filled, 1)
                pe.wait_ge(sem("merged"), KD * (g + 1))
                for n in range(KD):
                    out, w = begin("mix", (g, n)), weights()
                    product(out[:, 0:n_tok], lambda c: w[:, c, :], lambda c: merged[:, c, 0:n_tok], KD).then_inc(filled, 1)
                pe.wait_ge(sem("delta_t"), KD * (g + 1))
                for t in tiles:
                    _, at, rows = TILES[t]
                    for hf in range(2):
                        out = begin("x1", (t, hf))
                        for c in range(4):
                            ins = pe.transpose(out[0:rows, c * P:(c + 1) * P], hT[:, 4 * hf + c, at:at + rows], ident[:])
                        ins.then_inc(filled, 1)
                    pe.wait_ge(sem("h2_ready"), t + 1)
                    for hf in range(2):
                        out = begin("h2T", (t, hf))
                        for c in range(4):
                            f = (4 * hf + c) * P
                            ins = pe.transpose(out[:, c * P:c * P + rows], h2[0:rows, t, f:f + P], ident[0:rows, 0:rows])
                        ins.then_inc(filled, 1)
                pe.wait_ge(sem("h2_t"), 2 * (tiles[-1] + 1))
                for n in range(SEGS):
                    out, w = begin("query", (g, n)), weights()
                    product(out[:, 0:n_tok], lambda c: w[:, c, :], lambda c: merged[:, c, 0:n_tok], KD).then_inc(filled, 1)
                pe.wait_ge(sem("query_t"), SEGS * (g + 1))
                for t in tiles:
                    _, at, rows = TILES[t]
                    for j in range(4):
                        out = begin("keyscore", (t, j))
                        for i in range(4):
                            m = 4 * j + i
                            ins = pe.matmul(out[0:rows, i * P:(i + 1) * P], gates[:, m, at:at + rows],
                                            keys_t[:, m % 2, :], start=True, stop=True)
                        ins.then_inc(filled, 1)
                if g == 1:
                    for s in range(2):
                        _, n_seg, at = SEG[1][s]
                        at += n_seg - STATE
                        out = begin("state", s)
                        for c in range(KC):
                            ins = pe.transpose(out[0:STATE, c * P:(c + 1) * P], glu[:, c, at:at + STATE], ident[:])
                        ins.then_inc(filled, 1)

            for t, (_, at, rows) in enumerate(TILES):
                if t:
                    pe.wait_ge(sem("x2_ready"), t)
                else:
                    pe.wait_ge(sem("experts"), len(TILES))
                for hf in range(2):
                    pe.matmul(acc[:, hf * 512:(hf + 1) * 512], zeros[0:rows, :], x1[0:rows, t, hf * 512:(hf + 1) * 512],
                              start=True, stop=False, skip_group_check=True)
                with pe.Fori(0, ITERS) as i:
                    for half in range(2):
                        group = t * 2 * ITERS + half + i * 2
                        pe.wait_ge(sem("diag"), group + 1)
                        for k in range(HALF):
                            pe.wait_ge(v_loaded[k], (group + 1) * 16)
                            for hf in range(2):
                                ins = pe.matmul(acc[:, hf * 512:(hf + 1) * 512], diag[0:rows, half, k, :],
                                                vring[0:rows, k, hf * 512:(hf + 1) * 512],
                                                start=False, stop=False, skip_group_check=True)
                            ins.then_inc(v_free, 1)
                for hf in range(2):
                    ins = pe.matmul(acc[0:P, hf * 512:(hf + 1) * 512], ident[0:rows, :], x1[0:rows, t, hf * 512:(hf + 1) * 512],
                                    start=False, stop=True, skip_group_check=True)
                ins.then_inc(sem("acc_full"), 1)
                pe.wait_ge(sem("h3_ready"), t + 1)
                for hf in range(2):
                    out = begin("h3T", (t, hf))
                    for c in range(4):
                        f = (4 * hf + c) * P
                        ins = pe.transpose(out[:, c * P:c * P + rows], h3[0:rows, f:f + P], ident[0:rows, 0:rows])
                    ins.then_inc(filled, 1)
                if t == 0:
                    pe.wait_ge(loaded["tail"], 16 * 3)
                pe.wait_ge(sem("h3_t"), 2 * (t + 1))
                tok = START[TILES[t][0]] + at
                for hf in range(2):
                    f = slice(hf * 512, (hf + 1) * 512)
                    out = begin("ple_gate", (t, hf))
                    product(out[0:rows, :], lambda c: h3T[:, c, 0:rows], lambda c: w_pg[:, c, f], KD).then_inc(filled, 1)
                    out = begin("ple", (t, hf))
                    product(out[0:rows, :], lambda c: p_t[:, c, tok:tok + rows], lambda c: w_ple[:, c, f], KP).then_inc(filled, 1)

        @block.scalar
        def _(sc):
            ch = Chain(sc, sem("scalar_step"))

            def col(base, n=0):
                return cols[:, base + n:base + n + 1]

            sc.wait_ge(loaded["const"], 16 * 9)
            sc.wait_ge(loaded["cache"], 16 * 3)
            sc.wait_ge(sem("filled_const"), 4)
            for g in range(2):
                n_tok, tiles, cw = WIDTH[g], GROUPS[g], CONVW[g]
                sc.wait_ge(loaded[f"xT{g}"], 16)
                if g:
                    full(sc, "query", (0, SEGS - 1))
                ch.step(sc.activation(merged[:, :, 0:n_tok], hT[:, :, 0:n_tok], ACT.Square), "x_squared")
                full(sc, "ms", g)
                ch.step(sc.activation(tmp[:, 0:n_tok], bank("ms", g)[:, 0:n_tok], ACT.Sqrt, bias=eps[:, 0:1]), "rms_x")
                for n in SCALAR_Z:
                    full(sc, "z", (g, n))
                    src, b = bank("z", (g, n))[:, 0:n_tok], col(C_BIN, n)
                    if n < Q0:
                        if g:
                            sc.wait_ge(sem("glu"), KC)
                        ch.step(sc.activation(sig[:, n - KC, 0:n_tok], src, ACT.Sigmoid, bias=b), "scalar_z")
                    elif n < K0:
                        ch.step(sc.activation(qT[:, n - Q0, 0:n_tok], src, ACT.Identity, bias=b), "scalar_z")
                    elif n == K0:
                        if g:
                            ch.step(sc.activation(kT[:, KCOLS - DEC:KCOLS], src[:, 2 * P:n_tok], ACT.Identity, bias=b))
                        at = WINDOW + START[g]
                        ch.step(sc.activation(kT[:, at:at + 2 * P], src[:, 0:2 * P], ACT.Identity, bias=b), "scalar_z")
                    elif n == V0:
                        ch.step(sc.activation(vT[:, 0:n_tok], src, ACT.Identity, bias=b), "scalar_z")
                    else:
                        ch.step(sc.activation(gates[:, n - G0, 0:n_tok], src, ACT.Sigmoid, bias=b), "scalar_z")
                for t in tiles:
                    _, at, rows = TILES[t]
                    lo, hi = (P if t == 0 else 0), (2 * P if t < SAMPLE else WINDOW + DEC)
                    if t == GROUPS[1][0]:
                        sc.wait_ge(sem("experts"), len(GROUPS[0]))
                    for j in range(PAIRS):
                        full(sc, "score", (t, j))
                        src = bank("score", (t, j))[0:rows, :].rearrange("p (k s) -> p k s", k=KV)[:, :, lo:hi]
                        ch.step(sc.activation(S[0:rows, 2 * j:2 * j + 2, lo:hi], src, ACT.Copy, scale=HD ** -0.5), "scores")
                    sc.wait_ge(sem("score_max"), t + 1)
                    for h in range(H):
                        ch.step(sc.activation(S[0:rows, h, lo:hi], S[0:rows, h, lo:hi], ACT.Exp,
                                              bias=small[0:rows, h:h + 1], accum_out=small[0:rows, 16 + h:17 + h]))
                    ch.step(sc.activation(small[0:rows, 24:32], small[0:rows, 24:32], ACT.Exp), "exps")
                    for j in range(PAIRS):
                        full(sc, "probT", (t, j))
                        n_q = slice(0, rows)
                        src = bank("probT", (t, j)).rearrange("p (b q) -> p b q", b=4)
                        for kv in range(KV):
                            for part in range(lo // P, 2):
                                n_k = min((part + 1) * P, hi) - part * P
                                b = 2 * kv + part
                                last = kv == KV - 1 and part == 1
                                ch.step(sc.activation(PT[0:n_k, 4 * j + b, n_q], src[0:n_k, b, n_q], ACT.Copy),
                                        "probs_t" if last else None)
                    full(sc, "attT", t)
                    src = bank("attT", t).rearrange("p (j q) -> p j q", j=PAIRS)
                    ch.step(sc.activation(attT[:, :, at:at + rows], src[:, :, 0:rows], ACT.Copy), "att_t")
                sc.wait_ge(sem("centred"), g + 1)
                ch.step(sc.activation(convsq[:, :, 0:cw], conv[:, :, 0:cw], ACT.Square), "conv_squared")
                full(sc, "var", g)
                ch.step(sc.activation(rstd[:, 0:cw], bank("var", g)[:, 0:cw], ACT.Sqrt, bias=eps[:, 0:1]), "rms_conv")
                sc.wait_ge(sem("conv_normed"), g + 1)
                for c in range(KC):
                    for s, (tok, n_seg, at) in enumerate(SEG[g]):
                        last = c == KC - 1 and s == len(SEG[g]) - 1
                        ch.step(sc.activation(cT[:, c, tok:tok + n_seg], conv[:, c, at - STATE:at - STATE + n_seg],
                                              ACT.Silu, bias=col(C_BCLN, c), scale=col(C_GCLN, c)),
                                "silu" if last else None)
                for n in range(KD):
                    full(sc, "mix", (g, n))
                    ch.step(sc.activation(hT[:, n, 0:n_tok], bank("mix", (g, n))[:, 0:n_tok], ACT.Copy), "delta_t")
                for t in tiles:
                    _, at, rows = TILES[t]
                    sc.wait_ge(sem("x1_squares"), t + 1)
                    ch.step(sc.activation(small[0:rows, 33:34], small[0:rows, 32:33], ACT.Sqrt, scale=1.0 / D,
                                          bias=eps[0:rows, 0:1]), "rms_x1")
                    for hf in range(2):
                        full(sc, "h2T", (t, hf))
                        src = bank("h2T", (t, hf)).rearrange("p (c q) -> p c q", c=4)
                        ch.step(sc.activation(merged[:, 4 * hf:4 * hf + 4, at:at + rows], src[:, :, 0:rows], ACT.Copy), "h2_t")
                for n in range(SEGS):
                    full(sc, "query", (g, n))
                    ch.step(sc.activation(gates[:, n, 0:n_tok], bank("query", (g, n))[:, 0:n_tok], ACT.Copy), "query_t")
                for t in tiles:
                    rows = TILES[t][2]
                    sc.wait_ge(sem("probs"), tiles[-1] + 1)
                    if t > tiles[0]:
                        sc.wait_ge(sem("experts"), t)
                    for j in range(4):
                        full(sc, "keyscore", (t, j))
                        ch.step(sc.activation(S[0:rows, 2 * j:2 * j + 2, :].rearrange("p a b -> p (a b)"),
                                              bank("keyscore", (t, j))[0:rows, :], ACT.Copy), "key_scores")
                    sc.wait_ge(sem("top_ready"), t + 1)
                    ch.step(sc.activation(top[0:rows], top[0:rows], ACT.Exp), "top_exps")
                if g == 1:
                    for s in range(2):
                        full(sc, "state", s)
                        ch.step(sc.activation(stash[:, s, :], bank("state", s)[0:STATE, :], ACT.Copy), "conv_state")

            def root(name_in, name_out, t, rows):
                sc.wait_ge(sem(name_in), t + 1)
                ch.step(sc.activation(small[0:rows, 33:34], small[0:rows, 32:33], ACT.Sqrt, scale=1.0 / D,
                                      bias=eps[0:rows, 0:1]), name_out)

            for s in range(len(TILES) + 1):
                if s < len(TILES):
                    rows = TILES[s][2]
                    sc.wait_ge(sem("gelu_in"), s + 1)
                    ch.step(sc.activation(h3[0:rows, 0:PICKS], h3[0:rows, 0:PICKS], ACT.Tanh, scale=GELU_K), "gelu_tanh")
                if s:
                    t = s - 1
                    rows = TILES[t][2]
                    sc.wait_ge(sem("acc_full"), t + 1)
                    ch.step(sc.activation(x2[0:rows, :], acc[0:rows, :], ACT.Copy), "x2_ready")
                    root("x2_squares", "rms_x2", t, rows)
                    for hf in range(2):
                        full(sc, "h3T", (t, hf))
                        src = bank("h3T", (t, hf)).rearrange("p (c q) -> p c q", c=4)
                        ch.step(sc.activation(h3T[:, 4 * hf:4 * hf + 4, 0:rows], src[:, :, 0:rows], ACT.Copy), "h3_t")
                    for hf in range(2):
                        full(sc, "ple_gate", (t, hf))
                        ch.step(sc.activation(pgate[0:rows, hf * 512:(hf + 1) * 512], bank("ple_gate", (t, hf))[0:rows, :],
                                              ACT.Sigmoid), "ple_gate")
                    root("x3_squares", "rms_x3", t, rows)

        @block.vector
        def _(ve):
            ch = Chain(ve, sem("vector_step"))

            def col(base, n=0):
                return cols[:, base + n:base + n + 1]

            def normed(t, rows, out, src, gain, squares, rms, ready):
                ch.step(ve.tensor_tensor_reduce(out, src, src, 1.0, 0.0, ALU.mult, ALU.add, small[0:rows, 32:33]), squares)
                ve.wait_ge(sem(rms), t + 1)
                ch.step(ve.reciprocal(small[0:rows, 34:35], small[0:rows, 33:34]))
                ch.step(ve.scalar_tensor_tensor(out, src, small[0:rows, 34:35], gains[0:rows, gain, :], ALU.mult, ALU.mult), ready)

            for buf, value in ((over_d, 1.0 / D), (over_c, 1.0 / DC), (zeros, 0.0), (eps, EPS)):
                ve.memset(buf[:], value).then_inc(sem("filled_const"), 1)
            ve.memset(glu[:, :, 0:STATE], 0.0).then_inc(u_free, SLOTS)
            ve.memset(small[:], 0.0).then_inc(v_free, SLOTS + 1)
            ve.memset(dot[:], 0.0).then_inc(sem("dots_kept"), 1)
            ve.wait_ge(loaded["const"], 16 * 9)
            ve.wait_ge(loaded["cache"], 16 * 3)
            ve.wait_ge(u_free, SLOTS)
            ve.wait_ge(v_free, SLOTS + 1)
            for g in range(2):
                n_tok, tiles, cw = WIDTH[g], GROUPS[g], CONVW[g]
                ve.wait_ge(sem("rms_x"), g + 1)
                ch.step(ve.reciprocal(rstd[:, 0:n_tok], tmp[:, 0:n_tok]))
                for c in range(KD):
                    ch.step(ve.scalar_tensor_tensor(hT[:, c, 0:n_tok], hT[:, c, 0:n_tok], col(C_GMIX, c), rstd[:, 0:n_tok],
                                                    ALU.mult, ALU.mult), "h_ready" if c == KD - 1 else None)
                if g:
                    ch.step(ve.tensor_copy(glu[:, :, 0:STATE], glu[:, :, 2 * P:2 * P + STATE]))
                    ch.step(ve.tensor_copy(glu[:, :, 2 * P + STATE:2 * P + 2 * STATE], past[:]))
                for c in range(KC):
                    full(ve, "z", (g, c))
                    ve.wait_ge(sem("scalar_z"), len(SCALAR_Z) * g + c + 1)
                    for s, (tok, n_seg, at) in enumerate(SEG[g]):
                        ch.step(ve.scalar_tensor_tensor(glu[:, c, at:at + n_seg], bank("z", (g, c))[:, tok:tok + n_seg],
                                                        col(C_BIN, c), sig[:, c, tok:tok + n_seg], ALU.add, ALU.mult),
                                "glu" if s == len(SEG[g]) - 1 else None)
                for t in tiles:
                    rows = TILES[t][2]
                    full(ve, "vtok", t)
                    src = bank("vtok", t)
                    if t >= 3:
                        ch.step(ve.tensor_copy(ktok[0:rows, t - 3, :], src[0:rows, P:2 * P]))
                    ch.step(ve.tensor_copy(vtok[0:rows, t if t < SAMPLE else 5, :], src[0:rows, 0:P]), "tokens_v")
                base = KC * TAPS * g
                for w in range(TAPS):
                    for c in range(KC):
                        src, out = glu[:, c, w:w + cw], conv[:, c, 0:cw]
                        tap = col(C_WDW, c * TAPS + w)
                        if w == 0:
                            ve.tensor_scalar(out, src, tap, col(C_BDW, c), ALU.mult, ALU.add).then_inc(sem("conv"), 1)
                        else:
                            ve.wait_ge(sem("conv"), base + KC * (w - 1) + c + 1)
                            ve.scalar_tensor_tensor(out, src, tap, out, ALU.mult, ALU.add).then_inc(sem("conv"), 1)
                ve.wait_ge(sem("conv"), base + KC * TAPS)
                for t in tiles:
                    rows = TILES[t][2]
                    lo, hi = (P if t == 0 else 0), (2 * P if t < SAMPLE else WINDOW + DEC)
                    ve.wait_ge(sem("scores"), PAIRS * (t + 1))
                    for h in range(H):
                        ch.step(ve.scalar_tensor_tensor(S[0:rows, h, lo:hi], dist[0:rows, lo:hi], -SLOPES[h],
                                                        S[0:rows, h, lo:hi], ALU.mult, ALU.add))
                    ch.step(ve.tensor_reduce(small[0:rows, 8:16], S[0:rows, :, lo:hi], AX, ALU.max))
                    ch.step(ve.tensor_tensor(small[0:rows, 8:16], small[0:rows, 8:16], sinks[0:rows, :], ALU.max))
                    ch.step(ve.tensor_tensor(small[0:rows, 24:32], sinks[0:rows, :], small[0:rows, 8:16], ALU.subtract))
                    ch.step(ve.tensor_scalar(small[0:rows, 0:8], small[0:rows, 8:16], -1.0, None, ALU.mult), "score_max")
                    ve.wait_ge(sem("exps"), t + 1)
                    ch.step(ve.tensor_tensor(small[0:rows, 16:24], small[0:rows, 16:24], small[0:rows, 24:32], ALU.add))
                    ch.step(ve.reciprocal(small[0:rows, 16:24], small[0:rows, 16:24]))
                    ch.step(ve.tensor_tensor(S[0:rows, :, lo:hi], S[0:rows, :, lo:hi],
                                             small[0:rows, 16:24].unsqueeze(2).to_broadcast([rows, H, hi - lo]), ALU.mult), "probs")
                full(ve, "mean", g)
                for c in range(KC):
                    ch.step(ve.tensor_tensor(conv[:, c, 0:cw], conv[:, c, 0:cw], bank("mean", g)[:, 0:cw], ALU.subtract),
                            "centred" if c == KC - 1 else None)
                ve.wait_ge(sem("rms_conv"), g + 1)
                ch.step(ve.reciprocal(rstd[:, 0:cw], rstd[:, 0:cw]))
                ch.step(ve.tensor_tensor(conv[:, :, 0:cw], conv[:, :, 0:cw],
                                         rstd[:, 0:cw].unsqueeze(1).to_broadcast([P, KC, cw]), ALU.mult), "conv_normed")
                ve.wait_ge(sem("scalar_z"), len(SCALAR_Z) * (g + 1))
                for n in range(KD):
                    full(ve, "attn_out", (g, n))
                    ch.step(ve.scalar_tensor_tensor(merged[:, n, 0:n_tok], bank("conv_out", (g, n))[:, 0:n_tok], col(C_BCOUT, n),
                                                    gates[:, n, 0:n_tok], ALU.add, ALU.mult))
                    ch.step(ve.tensor_tensor(tmp[:, 0:n_tok], bank("attn_out", (g, n))[:, 0:n_tok],
                                             gates[:, KD + n, 0:n_tok], ALU.mult))
                    ch.step(ve.tensor_tensor(merged[:, n, 0:n_tok], merged[:, n, 0:n_tok], tmp[:, 0:n_tok], ALU.add), "merged")
                ve.wait_ge(loaded["x"], 32)
                for t in tiles:
                    rows = TILES[t][2]
                    for hf in range(2):
                        full(ve, "x1", (t, hf))
                        f = slice(hf * 512, (hf + 1) * 512)
                        ch.step(ve.tensor_tensor(x1[0:rows, t, f], bank("x1", (t, hf))[0:rows, :], x1[0:rows, t, f], ALU.add), "x1_ready")
                    normed(t, rows, h2[0:rows, t, :], x1[0:rows, t, :], 0, "x1_squares", "rms_x1", "h2_ready")
                for t in tiles:
                    rows = TILES[t][2]
                    ve.wait_ge(sem("key_scores"), 4 * (t + 1))
                    scores = S[0:rows].rearrange("p a b -> p (a b)").rearrange("p (m k) -> p m k", k=KEYS)
                    cand = PT[0:rows].rearrange("p a b -> p (a b)").rearrange("p (r k) -> p r k", r=HEADS)

                    def top16(values, vals, ids_out):
                        ch.step(ve.max(vals[:, 0:8], values))
                        ch.step(ve.max_index(ids_out[:, 0:8], vals[:, 0:8], values))
                        ch.step(ve.match_replace(values, vals[:, 0:8], values, LOWEST))
                        ch.step(ve.max(vals[:, 8:16], values))
                        ch.step(ve.max_index(ids_out[:, 8:16], vals[:, 8:16], values))

                    for m in range(SEGS):
                        top16(scores[:, m, :], best[0:rows, m, :], bestid[0:rows, m, :])
                    ch.step(ve.tensor_copy(bestidf[0:rows], bestid[0:rows]))
                    b = best[0:rows].rearrange("p (r two) k -> p r two k", two=2)
                    c4 = cand.rearrange("p r (i j) -> p r i j", i=TOPK)
                    for r in range(HEADS):
                        ch.step(ve.tensor_tensor(c4[:, r], b[:, r, 0, :].unsqueeze(2).to_broadcast([rows, TOPK, TOPK]),
                                                 b[:, r, 1, :].unsqueeze(1).to_broadcast([rows, TOPK, TOPK]), ALU.add))
                    for r in range(HEADS):
                        top16(cand[:, r, :], top[0:rows, r, :], pos[0:rows, 0, r, :])
                    ch.step(ve.tensor_copy(small[0:rows, 48:56], top[0:rows, :, 0]))
                    ch.step(ve.tensor_tensor(top[0:rows], top[0:rows], small[0:rows, 48:56].unsqueeze(2).to_broadcast([rows, HEADS, TOPK]),
                                             ALU.subtract), "top_ready")
                    ch.step(ve.tensor_scalar(pos[0:rows, 1], pos[0:rows, 0], 4, None, ALU.logical_shift_right))
                    ch.step(ve.tensor_scalar(pos[0:rows, 2], pos[0:rows, 0], TOPK - 1, None, ALU.bitwise_and))
                    ch.step(ve.tensor_copy(posf[0:rows], pos[0:rows, 1:3]))
                    bi = bestidf[0:rows].rearrange("p (r two) k -> p r two k", two=2)
                    for side in range(2):
                        for r in range(HEADS):
                            hot = cand[:, r, :].rearrange("p (k i) -> p k i", i=TOPK)
                            ch.step(ve.tensor_tensor(hot, posf[0:rows, side, r, :].unsqueeze(2).to_broadcast([rows, TOPK, TOPK]),
                                                     iota[0:rows].unsqueeze(1).to_broadcast([rows, TOPK, TOPK]), ALU.is_equal))
                            ch.step(ve.tensor_tensor(hot, hot, bi[:, r, side, :].unsqueeze(1).to_broadcast([rows, TOPK, TOPK]), ALU.mult))
                        ch.step(ve.tensor_reduce(chosen[0:rows, side, :], cand.rearrange("p r (k i) -> p (r k) i", i=TOPK),
                                                 AX, ALU.add))
                    ve.wait_ge(sem("top_exps"), t + 1)
                    ch.step(ve.tensor_reduce(small[0:rows, 40:48], top[0:rows], AX, ALU.add))
                    ch.step(ve.reciprocal(small[0:rows, 40:48], small[0:rows, 40:48]))
                    ch.step(ve.tensor_tensor(gate[0:rows, t * PICKS:(t + 1) * PICKS].rearrange("p (r k) -> p r k", r=HEADS),
                                             top[0:rows], small[0:rows, 40:48].unsqueeze(2).to_broadcast([rows, HEADS, TOPK]),
                                             ALU.mult))
                    ch.step(ve.scalar_tensor_tensor(expert[0:rows, t * PICKS:(t + 1) * PICKS], chosen[0:rows, 0, :], float(KEYS),
                                                    chosen[0:rows, 1, :], ALU.mult, ALU.add), "experts")

            u_seen = sem("dots_kept")
            ve.wait_ge(stored, 16 * 8)
            for s in range(len(TILES) + 1):
                u_rows = TILES[s][2] if s < len(TILES) else 0
                v_rows = TILES[s - 1][2] if s else 0
                with ve.Fori(0, ITERS) as i:
                    for half in range(2):
                        if u_rows:
                            group = s * 2 * ITERS + half + i * 2
                            ve.wait_ge(u_seen, group + 1)
                            for k in range(HALF):
                                ve.wait_ge(u_loaded[k], (group + 1) * 16)
                                row = uring[0:u_rows, k, :]
                                ve.tensor_tensor_reduce(row, row, h2[0:u_rows, s, :], 1.0, 0.0, ALU.mult, ALU.add,
                                                        astage[0:u_rows, k:k + 1]).then_inc(u_free, 1)
                            ve.wait_ge(u_free, (group + 2) * HALF)
                            ve.tensor_scalar(dot[0:u_rows, bass.ds(i * 2 * HALF + half * HALF, HALF)], astage[0:u_rows, :], 1.0, None,
                                             ALU.mult).then_inc(u_seen, 1)
                        if v_rows:
                            group = (s - 1) * 2 * ITERS + half + i * 2
                            ve.wait_ge(v_free, group * HALF + 1)
                            w = act[0:v_rows, bass.ds(i * 2 * HALF + half * HALF + (s - 1) % 2 * PICKS, HALF)]
                            ve.tensor_tensor(diag[0:v_rows, half], ident[0:v_rows].unsqueeze(1).to_broadcast([v_rows, HALF, P]),
                                             w.unsqueeze(2).to_broadcast([v_rows, HALF, P]), ALU.mult).then_inc(sem("diag"), 1)
                if u_rows:
                    ve.wait_ge(u_seen, (s + 1) * 2 * ITERS + 1)
                    d, g1 = dot[0:u_rows, :], gate[0:u_rows, s * PICKS:(s + 1) * PICKS]
                    th = h3[0:u_rows, 0:PICKS]
                    ch.step(ve.tensor_tensor(th, d, d, ALU.mult))
                    ch.step(ve.tensor_scalar(th, th, GELU_C, 1.0, ALU.mult, ALU.add))
                    ch.step(ve.tensor_tensor(th, th, d, ALU.mult), "gelu_in")
                    ch.step(ve.scalar_tensor_tensor(g1, g1, 0.5, d, ALU.mult, ALU.mult))
                    ve.wait_ge(sem("gelu_tanh"), s + 1)
                    to = act[0:u_rows, s % 2 * PICKS:(s % 2 + 1) * PICKS]
                    ch.step(ve.scalar_tensor_tensor(to, th, 1.0, g1, ALU.add, ALU.mult))
                if v_rows:
                    t, rows = s - 1, v_rows
                    ve.wait_ge(sem("x2_ready"), t + 1)
                    normed(t, rows, h3[0:rows, :], x2[0:rows, :], 1, "x2_squares", "rms_x2", "h3_ready")
                    for hf in range(2):
                        f = slice(hf * 512, (hf + 1) * 512)
                        ve.wait_ge(sem("ple_gate"), 2 * t + hf + 1)
                        full(ve, "ple", (t, hf))
                        ch.step(ve.tensor_tensor(pgate[0:rows, f], bank("ple", (t, hf))[0:rows, :], pgate[0:rows, f], ALU.mult), "x3_half")
                    ch.step(ve.tensor_tensor(x2[0:rows, :], x2[0:rows, :], pgate[0:rows, :], ALU.add))
                    if t >= 2:
                        ve.wait_ge(sem(f"y_stored{t % 2}"), 16 * (t // 2))
                    normed(t, rows, y[0:rows, t % 2, :], x2[0:rows, :], 2, "x3_squares", "rms_x3", "y_ready")

        @block.gpsimd
        def _(po):
            po.wait_ge(stored, 16 * 8)
            po.wait_ge(sem("experts"), len(TILES))
            turn = {0: po.alloc_register("u_turn"), 2: po.alloc_register("v_turn")}
            po.reg_mov(turn[0], 1)
            po.reg_mov(turn[2], 2)
            for s in range(len(TILES) + 1):
                u_rows = TILES[s][2] if s < len(TILES) else 0
                v_rows = TILES[s - 1][2] if s else 0
                streams = []
                if u_rows:
                    streams.append((s, u_rows, a["expert_u"], uring, u_loaded, u_free, 0, "u_ids"))
                if v_rows:
                    streams.append((s - 1, v_rows, a["expert_v"], vring, v_loaded, v_free, 2, "v_ids"))
                with po.Fori(0, ITERS) as i:
                    for half in range(2):
                        for t, rows, _, _, _, _, st, staged in streams:
                            group = t * 2 * ITERS + half + i * 2
                            po.tensor_copy(ids[0:rows, st + half, :],
                                           expert[0:rows, bass.ds(i * 2 * HALF + half * HALF + t * PICKS, HALF)]).then_inc(sem(staged), 1)
                        for t, rows, _, _, _, _, st, staged in streams:
                            group = t * 2 * ITERS + half + i * 2
                            po.wait_ge(sem(staged), group + 1)
                        for k in range(HALF):
                            for t, rows, table, ring_, landed, free, st, staged in streams:
                                group = t * 2 * ITERS + half + i * 2
                                po.wait_ge(free, turn[st])
                                po.reg_add(turn[st], turn[st], 1)
                                po.indirect_dma_start(ring_[0:rows, k, :], None, table,
                                                      bass.IndirectOffsetOnAxis(ap=ids[0:rows, st + half, k:k + 1], axis=0)).then_inc(landed[k], 16)


_OUTS = {"y_p": (SEQ, D), "y_s": (DEC, D), "nk_p": (WINDOW, KV * HD), "nv_p": (WINDOW, KV * HD), "nc_p": (STATE, DC),
         "nk_s": (WINDOW, KV * HD), "nv_s": (WINDOW, KV * HD), "nc_s": (STATE, DC)}


def _blocks(w, n, k):
    return np.ascontiguousarray(w.reshape(k, P, n, P).transpose(2, 1, 0, 3))


def _rows(w, k):
    return np.ascontiguousarray(w.reshape(k, P, -1).transpose(1, 0, 2))


def _column(v):
    return v.reshape(-1, P).T


def layout(i):
    i = {k: np.asarray(v) for k, v in i.items()}
    x = np.concatenate([i["x_prompt"][0], i["x_sample"][0]])
    pe = np.concatenate([i["p_prompt"][0, 0], i["p_sample"][0, 0]])
    heads = np.arange(H * HD).reshape(KV, PAIRS, HD).transpose(1, 0, 2).reshape(-1)
    order = np.arange(NZ * P)
    order[Q0 * P:K0 * P] = Q0 * P + heads
    w_in, b_in = i["w_in"][0][:, order], i["b_in"][0][order]
    w_br = np.concatenate([i["w_cout"][0], i["w_aout"][0][heads]])
    q, k = np.arange(P)[:, None], np.arange(2 * P)[None, :]
    first = q // CHUNK * CHUNK
    seen = (k >= first) & (k < first + WINDOW + CHUNK)
    dist = np.where(seen, np.abs(q + WINDOW - k), 1e32).astype(np.float32)
    cols = np.concatenate([
        _column(b_in), _column(i["g_mix"][0]), _column(i["b_dw"][0]), _column(i["g_cln"][0]), _column(i["b_cln"][0]),
        _column(i["b_cout"][0]), i["w_dw"][0].reshape(TAPS, KC, P).transpose(2, 1, 0).reshape(P, -1)], axis=1)
    keys = np.stack([i["sub_keys1"][0], i["sub_keys2"][0]])
    return {
        "x_t": _rows(x.T, KD), "x_p": i["x_prompt"][0], "x_s": i["x_sample"][0], "p_t": _rows(pe.T, KP),
        "cols": cols, "ident": np.eye(P, dtype=np.float32), "dist": dist,
        "iota": np.tile(np.arange(TOPK, dtype=np.float32), (P, 1)), "keys_t": keys.transpose(2, 0, 1),
        "sinks": i["sinks"], "g_ffn": i["g_ffn"], "g_ple": i["g_ple"], "g_final": i["g_final"][None],
        "cache_kt": i["cache_k"].reshape(WINDOW, P).T, "cache_k": i["cache_k"].reshape(WINDOW, P),
        "cache_v": i["cache_v"].reshape(WINDOW, P), "past_t": _rows(i["state_conv"][0, 0].T, KC),
        "w_in": _blocks(w_in, NZ, KD), "w_br": _blocks(w_br, KD, KD), "w_out": _blocks(i["w_out"][0], KD, KD),
        "w_query": _blocks(i["w_query"][0], SEGS, KD), "w_ple": _rows(i["w_ple"][0], KP), "w_pg": _rows(i["w_ple_gate"][0], KD),
        "expert_u": i["expert_u"][0], "expert_v": i["expert_v"][0],
    }


def kernel(**inputs):
    import concourse.bacc as bacc
    from concourse.bass_utils import run_bass_kernel_spmd

    arrays = {k: np.ascontiguousarray(v) for k, v in layout(inputs).items()}
    nc = bacc.Bacc("TRN2", target_bir_lowering=False, num_devices=1)
    a = {k: nc.dram_tensor(k, v.shape, F32, kind="ExternalInput").ap() for k, v in arrays.items()}
    a |= {k: nc.dram_tensor(k, s, F32, kind="ExternalOutput").ap() for k, s in _OUTS.items()}
    build(nc, a)
    r = run_bass_kernel_spmd(nc, [arrays], core_ids=[0]).results[0]
    kv = (1, 1, WINDOW, KV, HD)
    return (r["y_p"].reshape(1, SEQ, D), r["y_s"].reshape(1, DEC, D), r["nk_p"].reshape(kv), r["nv_p"].reshape(kv),
            r["nc_p"].reshape(1, 1, STATE, DC), r["nk_s"].reshape(kv), r["nv_s"].reshape(kv),
            r["nc_s"].reshape(1, 1, STATE, DC))
```

```python
from contextlib import ExitStack

import numpy as np

import concourse.bass as bass
from concourse import mybir

F32 = mybir.dt.float32
U32 = mybir.dt.uint32
ALU = mybir.AluOpType
ACT = mybir.ActivationFunctionType
AX = mybir.AxisListType.X

P = 128
D, DC, DP = 1024, 512, 256
KD, KC, KP = D // P, DC // P, DP // P
SEQ, DEC = 512, 64
TOK = SEQ + DEC
H, KV, HD = 8, 2, 64
PAIRS = H // KV
CHUNK, WINDOW = 64, 128
TAPS = 31
STATE = TAPS - 1
NZ = (2 * DC + H * HD + 2 * KV * HD + 2 * D) // P
HEADS, TOPK, KEYS = 8, 16, 128
SEGS = 2 * HEADS
PICKS = HEADS * TOPK
EPS = 1e-6
SLOPES = [2.0 ** (-8.0 * (h + 1) / H) for h in range(H)]
GELU_C, GELU_K = 0.044715, 0.7978845608028654
LOWEST = -3.0e38

ARENA = 30624
TILES = [(0, 0, P), (0, P, P), (1, 0, P), (1, P, P), (1, 2 * P, DEC)]
GROUPS = [[t for t in range(len(TILES)) if TILES[t][0] == g] for g in range(2)]
WIDTH = [sum(TILES[t][2] for t in GROUPS[g]) for g in range(2)]
WMAX = max(WIDTH)
START = [0, WIDTH[0]]
SAMPLE = len(TILES) - 1
Q0, K0, V0, G0 = 2 * KC, 2 * KC + 4, 2 * KC + 5, 2 * KC + 6
ZORDER = [n for c in range(KC) for n in (KC + c, c)] + [K0, V0] + list(range(Q0, K0)) + list(range(G0, NZ))
SCALAR_Z = [n for n in ZORDER if n >= KC]
SEG = [[(0, 2 * P, STATE)], [(0, 2 * P, STATE), (2 * P, DEC, 2 * STATE + 2 * P)]]
CONVW = [2 * P, 2 * P + STATE + DEC]
GLUW = 2 * STATE + 2 * P + DEC
KCOLS = WINDOW + SEQ + WINDOW + DEC

BANKS = 4
WSLOTS = 4
USLOTS = 7
VSLOTS = 8
DIAGS = 16
GATHERS = [PICKS] * 4 + [PICKS // 2]
COLUMN = [t * PICKS for t in range(5)]
U_LIST = [(t, j) for t in range(5) for j in range(GATHERS[t])]
V_LIST = [(t, j) for t in range(5) for j in range(GATHERS[t])]
PHASE1 = GATHERS[0] + GATHERS[1]
BEATS = len(V_LIST)
FIRST = [sum(GATHERS[:t]) for t in range(6)]


def by_vector(t, j):
    return t < SAMPLE and j % 4 == 3


V_VECTOR = [n for n, (t, j) in enumerate(V_LIST) if by_vector(t, j)]
V_TENSOR = [n for n, (t, j) in enumerate(V_LIST) if not by_vector(t, j)]
V_ORDINAL = {n: k for part in (V_VECTOR, V_TENSOR) for k, n in enumerate(part)}

HOOKS = {"sum": 4, "root2": 6, "h3": 8, "h3T": 10, "h3T_copy": 12, "ple": 14, "sigmoid": 18, "x3": 21, "root3": 23, "y": 25}
CHOICE = {3: (0, 66, 68), 4: (58, 122, 124)}
CHOICE_STRIDE = 2
GELU_AHEAD = 30


def attention_order(tiles):
    a, b, *c = tiles
    return [("s", a), ("s", b), ("e", a), ("e", b), ("p", a)] + [(k, t) for t in c for k in "se"] + [("p", t) for t in (b, *c)]


DOTS_PER_US = 1.1
C_BIN, C_GMIX, C_BDW, C_GCLN, C_BCLN, C_BCOUT, C_WDW = 0, 30, 38, 42, 46, 50, 58
NCOLS = C_WDW + KC * TAPS


def plan_units():
    units, count = [], {}

    def unit(name, key, sem, step=1):
        count[sem] = count.get(sem, 0) + step
        units.append((name, key, sem, count[sem]))

    for g in range(2):
        unit("ms", g, "rms_x")
        for n in ZORDER:
            unit("z", (g, n), "scalar_z" if n >= KC else "glu")
        for t in GROUPS[g]:
            unit("vtok", t, "tokens_v")
        for stage, t in attention_order(GROUPS[g]):
            if stage == "s":
                for j in range(PAIRS):
                    unit("score", (t, j), "scores")
            if stage == "p":
                for j in range(PAIRS):
                    unit("probT", (t, j), "probs_t")
                unit("attT", t, "att_t")
        unit("mean", g, "centred")
        unit("var", g, "rms_conv")
        for n in range(KD):
            unit("conv_out", (g, n), "merged", 1)
            unit("attn_out", (g, n), "merged", 0)
        for n in range(KD):
            unit("mix", (g, n), "delta_t")
        for t in GROUPS[g]:
            for hf in range(2):
                unit("x1", (t, hf), "x1_ready")
            for hf in range(2):
                unit("h2T", (t, hf), "h2_t")
        for n in range(SEGS):
            unit("query", (g, n), "query_t")
        for t in GROUPS[g]:
            for j in range(4):
                unit("keyscore", (t, j), "key_scores")
        if g == 1:
            for s in range(2):
                unit("state", s, "conv_state")
    for t in range(len(TILES)):
        for hf in range(2):
            unit("h3T", (t, hf), "h3_t")
        for hf in range(2):
            unit("ple_gate", (t, hf), "ple_gate")
            unit("ple", (t, hf), "x3_half")
    return units


UNITS = plan_units()
AT = {(name, key): u for u, (name, key, _, _) in enumerate(UNITS)}
WEIGHTS = [
    (what, n, AT[unit, (g, n)])
    for g in range(2)
    for what, unit, order in (("w_in", "z", ZORDER), ("w_br", "attn_out", range(KD)),
                              ("w_out", "mix", range(KD)), ("w_query", "query", range(SEGS)))
    for n in order
]


def build(nc, a):
    ctx = ExitStack()

    def sb(name, shape, dt=F32, stack=None):
        return (stack or ctx).enter_context(nc.sbuf_tensor(f"{name}_buf", shape, dt))

    with ctx:
        cols = sb("cols", [P, NCOLS])
        g_ffn = sb("g_ffn", [P, D])
        ident = sb("ident", [P, P])
        fold = sb("fold", [P, DEC])
        sinks = sb("sinks", [P, H])
        dist = sb("dist", [P, 2 * P])
        iota = sb("iota", [P, TOPK])
        keys_t = sb("keys_t", [P, 2, KEYS])
        over_d = sb("over_d", [P, P])
        over_c = sb("over_c", [P, P])
        eps = sb("eps", [P, 1])
        x1 = sb("x1", [P, len(TILES), D])
        h2 = sb("h2", [P, len(TILES), D])
        expert = sb("expert", [P, len(TILES) * PICKS], U32)
        gate = sb("gate", [P, len(TILES) * PICKS])
        dot = sb("dot", [P, len(TILES) * PICKS])
        tanh = sb("tanh", [P, PICKS])
        small = sb("small", [P, 2, 32])
        stat = sb("stat", [P, 32])
        uring = sb("uring", [P, USLOTS, D])

        arena = sb("arena", [P, ARENA])
        used = [0]

        def take(*shape, dt=F32, at=None):
            n = int(np.prod(shape))
            if at is not None:
                used[0] = at
            view = arena[:, used[0]:used[0] + n]
            used[0] += n
            assert used[0] <= ARENA, used[0]
            if dt != F32:
                view = view.bitcast(dt)
            names = "abcd"[:len(shape)]
            return view.rearrange(f"p ({' '.join(names)}) -> p {' '.join(names)}", **dict(zip(names, shape))) if len(shape) > 1 else view

        wring = take(WSLOTS, KD, P, at=0)
        gates = take(SEGS, WMAX)
        assert used[0] <= VSLOTS * D + DIAGS * P
        used[0] = VSLOTS * D + DIAGS * P - GLUW
        rstd = take(GLUW)
        assert used[0] - GLUW >= WSLOTS * KD * P + SEGS * WMAX
        late = used[0]
        sig = take(KC, WMAX)
        qT = take(PAIRS, WMAX)
        kT = take(KCOLS)
        vT = take(WMAX)
        tmp = take(WMAX)
        vtok = take(6, P)
        ktok = take(2, P)
        glu = take(KC, GLUW)
        conv = take(KC, CONVW[1])
        past = take(KC, STATE)
        attT = take(PAIRS, WMAX)
        hT = take(KD, WMAX)
        merged = take(KD, WMAX)
        used_trunk = used[0]
        S0 = take(H * 2 * P)
        PT = take(H * 2, P)
        best = take(SEGS, TOPK)
        bestid = take(SEGS, TOPK, dt=U32)
        bestidf = take(SEGS, TOPK)
        top = take(HEADS, TOPK)
        pos = take(3 * HEADS, TOPK, dt=U32)
        posf = take(2 * HEADS, TOPK)
        chosen = take(2, PICKS)
        hT_at, merged_at = used_trunk - 2 * KD * WMAX, used_trunk - KD * WMAX
        S1 = take(H * 2 * P, at=hT_at)
        S2 = take(H * 2 * P, at=merged_at)
        convsq = take(KC, CONVW[1], at=merged_at)
        stash = sig.rearrange("p a b -> p (a b)")[0:STATE, 0:2 * DC].rearrange("p (s c) -> p s c", s=2)
        cT = sig
        att_S = [b.rearrange("p (h s) -> p h s", h=H) for b in (S0, S1)]
        key_S = {t: b.rearrange("p (m k) -> p m k", k=KEYS) for t, b in zip(range(5), (S0, S1, S0, S1, S2))}
        vring = take(VSLOTS, D, at=0)
        diag = take(DIAGS, P)
        assert used[0] <= late
        w_pg = take(KD, D, at=late)
        w_ple = take(KP, D)
        p_t = take(KP, TOK)
        gains = take(2, D)
        h3 = take(D)
        h3T = take(KD, P)
        pgate = take(D)
        y = take(2, D)

        ring = [ctx.enter_context(nc.psum_tensor(f"ring{b}", [P, 512], F32)) for b in range(BANKS)]
        acc = [ctx.enter_context(nc.psum_tensor(f"acc{b}", [P, D], F32)) for b in range(2)]

        sems = {}

        def sem(name):
            if name not in sems:
                sems[name] = ctx.enter_context(nc.semaphore(name))
            return sems[name]

        filled = sem("filled")
        loaded = {k: sem(f"loaded_{k}") for k in ("const", "xT0", "xT1", "x", "late", "cache", "h2_fold", "id_fold")}
        w_loaded = [sem(f"w_loaded{i}") for i in range(WSLOTS)]
        u_loaded = [sem(f"u_loaded{i}") for i in range(USLOTS)]
        v_loaded = [sem(f"v_loaded{i}") for i in range(VSLOTS)]
        u_used, v_tensor, v_vector = sem("u_used"), sem("v_tensor"), sem("v_vector")
        stored = sem("stored")

        block = ctx.enter_context(nc.Block())

        def bank(name, key):
            return ring[AT[name, key] % BANKS]

        def full(eng, name, key):
            eng.wait_ge(filled, AT[name, key] + 1)

        class Chain:

            def __init__(self, eng, own):
                self.eng, self.own, self.count, self.last = eng, own, {}, None

            def go(self, ins, name=None):
                s = sem(name) if name else self.own
                self.count[s] = self.count.get(s, 0) + 1
                ins.then_inc(s, 1)
                self.last = s

            def settle(self):
                self.eng.wait_ge(self.last, self.count[self.last])

            def step(self, ins, name=None):
                self.go(ins, name)
                self.settle()

            def lag(self, make, n):
                c = self.count.get(self.own, 0)
                if c - n + 1 > 0:
                    self.eng.wait_ge(self.own, c - n + 1)
                self.go(make())

        def last_stage(n, parts):
            for t in range(SAMPLE):
                for part, do in parts.items():
                    if n == FIRST[t + 1] + HOOKS[part]:
                        do(t)

        @block.sync
        def _(sp):
            sp.dma_start(hT[:, :, 0:WIDTH[0]], a["x_t"][:, :, 0:WIDTH[0]]).then_inc(loaded["xT0"], 16)
            for name, to in (("cols", cols), ("ident", ident), ("dist", dist), ("iota", iota), ("keys_t", keys_t)):
                sp.dma_start(to[:], a[name]).then_inc(loaded["const"], 16)
            sp.dma_start(sinks[:], a["sinks"].to_broadcast([P, H])).then_inc(loaded["const"], 16)
            sp.dma_start(fold[:], a["fold"]).then_inc(loaded["const"], 16)
            sp.dma_start(g_ffn[:], a["g_ffn"].to_broadcast([P, D])).then_inc(loaded["const"], 16)
            sp.dma_start(kT[:, WINDOW + SEQ:2 * WINDOW + SEQ], a["cache_kt"]).then_inc(loaded["cache"], 16)
            sp.dma_start(vtok[:, 4, :], a["cache_v"]).then_inc(loaded["cache"], 16)
            sp.dma_start(past[:], a["past_t"]).then_inc(loaded["cache"], 16)

            def extra(i):
                if i == 8:
                    sp.dma_start(x1[:, 0:4, :], a["x_p"].rearrange("(t p) d -> p t d", p=P)).then_inc(loaded["x"], 16)
                    sp.dma_start(x1[0:DEC, 4, :], a["x_s"]).then_inc(loaded["x"], 16)
                    sp.dma_start(a["nk_s"][0:DEC, :], a["cache_k"][DEC:WINDOW, :]).then_inc(stored, 16)
                    sp.dma_start(a["nv_s"][0:DEC, :], a["cache_v"][DEC:WINDOW, :]).then_inc(stored, 16)
                if i == len(WEIGHTS) // 2:
                    full(sp, "x1", (GROUPS[0][-1], 1))
                    sp.wait_ge(sem("experts"), len(GROUPS[0]))
                    sp.dma_start(hT[:, :, 0:WIDTH[1]], a["x_t"][:, :, WIDTH[0]:TOK]).then_inc(loaded["xT1"], 16)

            for i, (what, n, _) in enumerate(WEIGHTS):
                extra(i)
                if i >= WSLOTS:
                    sp.wait_ge(filled, WEIGHTS[i - WSLOTS][2] + 1)
                sp.dma_start(wring[:, i % WSLOTS], a[what][n]).then_inc(w_loaded[i % WSLOTS], 16)
            sp.wait_ge(sem("tokens_v"), 5)
            for t, rows, nk, nv, at in ((3, P, "nk_p", "nv_p", 0), (4, DEC, "nk_s", "nv_s", DEC)):
                sp.dma_start(a[nk][at:at + rows, :], ktok[0:rows, t - 3, :]).then_inc(stored, 16)
                sp.dma_start(a[nv][at:at + rows, :], vtok[0:rows, 3 if t == 3 else 5, :]).then_inc(stored, 16)
            sp.wait_ge(sem("conv_state"), 2)
            for s, name in enumerate(("nc_p", "nc_s")):
                sp.dma_start(a[name], stash[:, s, :]).then_inc(stored, 16)
            sp.wait_ge(sem("h2_ready"), len(TILES))
            sp.dma_start(h2[DEC:P, SAMPLE, :], h2[0:DEC, SAMPLE, :]).then_inc(loaded["h2_fold"], 16)
            sp.wait_ge(sem("experts"), len(TILES))
            sp.wait_ge(stored, 16 * 8)
            c = COLUMN[SAMPLE]
            for table in (expert, gate):
                sp.dma_start(table[DEC:P, c:c + PICKS // 2], table[0:DEC, c + PICKS // 2:c + PICKS]).then_inc(loaded["id_fold"], 16)
            for name, to in (("w_pg", w_pg), ("w_ple", w_ple), ("p_t", p_t)):
                sp.dma_start(to, a[name]).then_inc(loaded["late"], 16)
            for i, name in enumerate(("g_ple", "g_final")):
                sp.dma_start(gains[:, i, :], a[name].to_broadcast([P, D])).then_inc(loaded["late"], 16)
            for t, (g, at, rows) in enumerate(TILES):
                sp.wait_ge(sem("y_ready"), t + 1)
                to = a["y_p"][t * P:(t + 1) * P, :] if t < 4 else a["y_s"]
                sp.dma_start(to, y[0:rows, t % 2, :]).then_inc(sem(f"y_stored{t % 2}"), 16)
            sp.wait_ge(sem("y_stored0"), 16 * 3)
            sp.wait_ge(sem("y_stored1"), 16 * 2)

        @block.tensor
        def _(pe):
            wi = [0]

            def begin(name, key):
                u = AT[name, key]
                if u >= BANKS:
                    pe.wait_ge(sem(UNITS[u - BANKS][2]), UNITS[u - BANKS][3])
                return ring[u % BANKS]

            def weights():
                i = wi[0]
                wi[0] += 1
                pe.wait_ge(w_loaded[i % WSLOTS], 16 * (i // WSLOTS + 1))
                return wring[:, i % WSLOTS]

            def product(out, w, x, ks, last=None):
                for c in range(ks):
                    ins = pe.matmul(out, w(c), x(c), start=(c == 0), stop=(c == ks - 1))
                return ins

            pe.wait_ge(loaded["const"], 16 * 8)
            pe.wait_ge(loaded["cache"], 16 * 3)
            pe.wait_ge(sem("filled_const"), 3)
            for g in range(2):
                n_tok, tiles, cw = WIDTH[g], GROUPS[g], CONVW[g]
                pe.wait_ge(sem("x_squared"), g + 1)
                out = begin("ms", g)
                product(out[:, 0:n_tok], lambda c: over_d[:], lambda c: merged[:, c, 0:n_tok], KD).then_inc(filled, 1)
                pe.wait_ge(sem("h_ready"), g + 1)
                for n in ZORDER:
                    out, w = begin("z", (g, n)), weights()
                    product(out[:, 0:n_tok], lambda c: w[:, c, :], lambda c: hT[:, c, 0:n_tok], KD).then_inc(filled, 1)
                zdone = len(SCALAR_Z) * g
                pe.wait_ge(sem("scalar_z"), zdone + SCALAR_Z.index(V0) + 1)
                for t in tiles:
                    _, at, rows = TILES[t]
                    kat = WINDOW + t * P if t < SAMPLE else KCOLS - DEC
                    out = begin("vtok", t)
                    pe.transpose(out[0:rows, 0:P], vT[:, at:at + rows], ident[:])
                    pe.transpose(out[0:rows, P:2 * P], kT[:, kat:kat + rows], ident[:]).then_inc(filled, 1)
                pe.wait_ge(sem("scalar_z"), zdone + SCALAR_Z.index(K0 - 1) + 1)
                for stage, t in attention_order(tiles):
                    _, at, rows = TILES[t]
                    lo, hi = (P if t == 0 else 0), (2 * P if t < SAMPLE else WINDOW + DEC)
                    band = t * P if t < SAMPLE else WINDOW + SEQ
                    S = att_S[t % 2]
                    if stage == "s":
                        for j in range(PAIRS):
                            out = begin("score", (t, j))
                            f = slice(j // 2 * HD, (j // 2 + 1) * HD)
                            for b in range(2):
                                ins = pe.matmul(out[0:rows, b * 2 * P + lo:b * 2 * P + hi], qT[f, j % 2 * 2 + b, at:at + rows],
                                                kT[f, band + lo:band + hi], start=True, stop=True)
                            ins.then_inc(filled, 1)
                    if stage == "p":
                        pe.wait_ge(sem("probs"), t + 1)
                        for j in range(PAIRS):
                            out = begin("probT", (t, j))
                            for kv in range(KV):
                                for part in range(lo // P, 2):
                                    a0, a1 = part * P, min((part + 1) * P, hi)
                                    b = (2 * kv + part) * P
                                    ins = pe.transpose(out[0:a1 - a0, b:b + rows], S[0:rows, PAIRS * kv + j, a0:a1],
                                                       ident[0:rows, 0:rows])
                            ins.then_inc(filled, 1)
                        pe.wait_ge(sem("probs_t"), PAIRS * (t + 1))
                        pe.wait_ge(sem("tokens_v"), t + 1)
                        out = begin("attT", t)
                        for j in range(PAIRS):
                            for kv in range(KV):
                                for part in range(lo // P, 2):
                                    n_k = min((part + 1) * P, hi) - part * P
                                    vt = t - 1 + part if t < SAMPLE else 4 + part
                                    ins = pe.matmul(out[kv * HD:(kv + 1) * HD, j * P:j * P + rows],
                                                    vtok[0:n_k, vt, kv * HD:(kv + 1) * HD],
                                                    PT[0:n_k, 4 * j + 2 * kv + part, 0:rows],
                                                    start=(part == lo // P), stop=(part == 1))
                        ins.then_inc(filled, 1)
                pe.wait_ge(sem("conv"), KC * TAPS * (g + 1))
                out = begin("mean", g)
                product(out[:, 0:cw], lambda c: over_c[:], lambda c: conv[:, c, 0:cw], KC).then_inc(filled, 1)
                pe.wait_ge(sem("conv_squared"), g + 1)
                out = begin("var", g)
                product(out[:, 0:cw], lambda c: over_c[:], lambda c: convsq[:, c, 0:cw], KC).then_inc(filled, 1)
                pe.wait_ge(sem("silu"), g + 1)
                pe.wait_ge(sem("att_t"), tiles[-1] + 1)
                for n in range(KD):
                    out, w = begin("conv_out", (g, n)), weights()
                    product(out[:, 0:n_tok], lambda c: w[:, c, :], lambda c: cT[:, c, 0:n_tok], KC).then_inc(filled, 1)
                    out = begin("attn_out", (g, n))
                    product(out[:, 0:n_tok], lambda c: w[:, KC + c, :], lambda c: attT[:, c, 0:n_tok], KC).then_inc(filled, 1)
                pe.wait_ge(sem("merged"), KD * (g + 1))
                for n in range(KD):
                    out, w = begin("mix", (g, n)), weights()
                    product(out[:, 0:n_tok], lambda c: w[:, c, :], lambda c: merged[:, c, 0:n_tok], KD).then_inc(filled, 1)
                pe.wait_ge(sem("delta_t"), KD * (g + 1))
                for t in tiles:
                    _, at, rows = TILES[t]
                    for hf in range(2):
                        out = begin("x1", (t, hf))
                        for c in range(4):
                            ins = pe.transpose(out[0:rows, c * P:(c + 1) * P], hT[:, 4 * hf + c, at:at + rows], ident[:])
                        ins.then_inc(filled, 1)
                    pe.wait_ge(sem("h2_ready"), t + 1)
                    for hf in range(2):
                        out = begin("h2T", (t, hf))
                        for c in range(4):
                            f = (4 * hf + c) * P
                            ins = pe.transpose(out[:, c * P:c * P + rows], h2[0:rows, t, f:f + P], ident[0:rows, 0:rows])
                        ins.then_inc(filled, 1)
                pe.wait_ge(sem("h2_t"), 2 * (tiles[-1] + 1))
                for n in range(SEGS):
                    out, w = begin("query", (g, n)), weights()
                    product(out[:, 0:n_tok], lambda c: w[:, c, :], lambda c: merged[:, c, 0:n_tok], KD).then_inc(filled, 1)
                pe.wait_ge(sem("query_t"), SEGS * (g + 1))
                for t in tiles:
                    _, at, rows = TILES[t]
                    for j in range(4):
                        out = begin("keyscore", (t, j))
                        for i in range(4):
                            m = 4 * j + i
                            ins = pe.matmul(out[0:rows, i * P:(i + 1) * P], gates[:, m, at:at + rows],
                                            keys_t[:, m % 2, :], start=True, stop=True)
                        ins.then_inc(filled, 1)
                if g == 1:
                    for s in range(2):
                        _, n_seg, at = SEG[1][s]
                        at += n_seg - STATE
                        out = begin("state", s)
                        for c in range(KC):
                            ins = pe.transpose(out[0:STATE, c * P:(c + 1) * P], glu[:, c, at:at + STATE], ident[:])
                        ins.then_inc(filled, 1)

            def turn_h3(t):
                rows = TILES[t][2]
                pe.wait_ge(sem("h3_ready"), t + 1)
                for hf in range(2):
                    out = begin("h3T", (t, hf))
                    for c in range(4):
                        f = (4 * hf + c) * P
                        ins = pe.transpose(out[:, c * P:c * P + rows], h3[0:rows, f:f + P], ident[0:rows, 0:rows])
                    ins.then_inc(filled, 1)

            def ple(t):
                _, at, rows = TILES[t]
                pe.wait_ge(loaded["late"], 16 * 5)
                pe.wait_ge(sem("h3_t"), 2 * (t + 1))
                tok = START[TILES[t][0]] + at
                for hf in range(2):
                    f = slice(hf * 512, (hf + 1) * 512)
                    out = begin("ple_gate", (t, hf))
                    product(out[0:rows, :], lambda c: h3T[:, c, 0:rows], lambda c: w_pg[:, c, f], KD).then_inc(filled, 1)
                    out = begin("ple", (t, hf))
                    product(out[0:rows, :], lambda c: p_t[:, c, tok:tok + rows], lambda c: w_ple[:, c, f], KP).then_inc(filled, 1)

            for n, (t, j) in enumerate(V_LIST):
                last_stage(n, {"h3T": turn_h3, "ple": ple})
                if by_vector(t, j):
                    continue
                if j == 0 and t >= 2:
                    pe.wait_ge(sem("x2_ready"), t - 1)
                k = V_ORDINAL[n]
                last = j == GATHERS[t] - (2 if t < SAMPLE else 1)
                pe.wait_ge(v_loaded[n % VSLOTS], 16 * (n // VSLOTS + 1))
                pe.wait_ge(sem("diag"), k + 1)
                m = P if t < SAMPLE else DEC
                for hf in range(2):
                    f = slice(hf * 512, (hf + 1) * 512)
                    ins = pe.matmul(acc[t % 2][0:m, f], diag[:, k % DIAGS, 0:m], vring[:, n % VSLOTS, f],
                                    start=(j == 0), stop=last)
                ins.then_inc(v_tensor, 1)
            turn_h3(SAMPLE)
            ple(SAMPLE)

        @block.scalar
        def _(sc):
            ch = Chain(sc, sem("scalar_step"))

            def col(base, n=0):
                return cols[:, base + n:base + n + 1]

            def root(name_in, name_out, t):
                rows = TILES[t][2]
                sc.wait_ge(sem(name_in), t + 1)
                ch.go(sc.activation(stat[0:rows, 1:2], stat[0:rows, 0:1], ACT.Sqrt, scale=1.0 / D,
                                    bias=eps[0:rows, 0:1]), name_out)

            def top_exps(t):
                rows = TILES[t][2]
                sc.wait_ge(sem("top_ready"), t + 1)
                ch.go(sc.activation(top[0:rows], top[0:rows], ACT.Exp), "top_exps")

            sc.wait_ge(loaded["const"], 16 * 8)
            sc.wait_ge(loaded["cache"], 16 * 3)
            sc.wait_ge(sem("filled_const"), 3)
            for g in range(2):
                n_tok, tiles, cw = WIDTH[g], GROUPS[g], CONVW[g]
                sc.wait_ge(loaded[f"xT{g}"], 16)
                if g:
                    full(sc, "query", (0, SEGS - 1))
                ch.step(sc.activation(merged[:, :, 0:n_tok], hT[:, :, 0:n_tok], ACT.Square), "x_squared")
                full(sc, "ms", g)
                ch.step(sc.activation(tmp[:, 0:n_tok], bank("ms", g)[:, 0:n_tok], ACT.Sqrt, bias=eps[:, 0:1]), "rms_x")
                for n in SCALAR_Z:
                    full(sc, "z", (g, n))
                    src, b = bank("z", (g, n))[:, 0:n_tok], col(C_BIN, n)
                    if n < Q0:
                        if g:
                            sc.wait_ge(sem("glu"), KC)
                        ch.step(sc.activation(sig[:, n - KC, 0:n_tok], src, ACT.Sigmoid, bias=b), "scalar_z")
                    elif n < K0:
                        ch.step(sc.activation(qT[:, n - Q0, 0:n_tok], src, ACT.Identity, bias=b), "scalar_z")
                    elif n == K0:
                        if g:
                            ch.step(sc.activation(kT[:, KCOLS - DEC:KCOLS], src[:, 2 * P:n_tok], ACT.Identity, bias=b))
                        at = WINDOW + START[g]
                        ch.step(sc.activation(kT[:, at:at + 2 * P], src[:, 0:2 * P], ACT.Identity, bias=b), "scalar_z")
                    elif n == V0:
                        ch.step(sc.activation(vT[:, 0:n_tok], src, ACT.Identity, bias=b), "scalar_z")
                    else:
                        ch.step(sc.activation(gates[:, n - G0, 0:n_tok], src, ACT.Sigmoid, bias=b), "scalar_z")
                for stage, t in attention_order(tiles):
                    _, at, rows = TILES[t]
                    lo, hi = (P if t == 0 else 0), (2 * P if t < SAMPLE else WINDOW + DEC)
                    S, sm = att_S[t % 2], small[0:rows, t % 2, :]
                    if stage == "s":
                        if t == GROUPS[1][0]:
                            sc.wait_ge(sem("experts"), len(GROUPS[0]))
                        for j in range(PAIRS):
                            full(sc, "score", (t, j))
                            src = bank("score", (t, j))[0:rows, :].rearrange("p (k s) -> p k s", k=KV)[:, :, lo:hi]
                            ch.go(sc.activation(S[0:rows, 2 * j:2 * j + 2, lo:hi], src, ACT.Copy, scale=HD ** -0.5), "scores")
                    if stage == "e":
                        sc.wait_ge(sem("score_max"), t + 1)
                        for h in range(H):
                            ch.go(sc.activation(S[0:rows, h, lo:hi], S[0:rows, h, lo:hi], ACT.Exp,
                                                bias=sm[:, h:h + 1], accum_out=sm[:, 16 + h:17 + h]))
                        ch.go(sc.activation(sm[:, 24:32], sm[:, 24:32], ACT.Exp), "exps")
                    if stage == "p":
                        for j in range(PAIRS):
                            full(sc, "probT", (t, j))
                            src = bank("probT", (t, j)).rearrange("p (b q) -> p b q", b=4)
                            if t < SAMPLE:
                                part = slice(lo // P, 4, 1 + lo // P)
                                to = PT[:, 4 * j:4 * j + 4, :]
                                ch.go(sc.activation(to[:, part, :], src[:, part, :], ACT.Copy), "probs_t")
                            else:
                                to = PT[:, 4 * j:4 * j + 4, 0:rows]
                                ch.go(sc.activation(to[:, 0::2, :], src[:, 0::2, 0:rows], ACT.Copy))
                                ch.go(sc.activation(to[0:DEC, 1::2, :], src[0:DEC, 1::2, 0:rows], ACT.Copy), "probs_t")
                        full(sc, "attT", t)
                        src = bank("attT", t).rearrange("p (j q) -> p j q", j=PAIRS)
                        ch.go(sc.activation(attT[:, :, at:at + rows], src[:, :, 0:rows], ACT.Copy), "att_t")
                sc.wait_ge(sem("centred"), g + 1)
                ch.step(sc.activation(convsq[:, :, 0:cw], conv[:, :, 0:cw], ACT.Square), "conv_squared")
                full(sc, "var", g)
                ch.step(sc.activation(rstd[:, 0:cw], bank("var", g)[:, 0:cw], ACT.Sqrt, bias=eps[:, 0:1]), "rms_conv")
                sc.wait_ge(sem("conv_normed"), g + 1)
                for c in range(KC):
                    for s, (tok, n_seg, at) in enumerate(SEG[g]):
                        last = c == KC - 1 and s == len(SEG[g]) - 1
                        ch.step(sc.activation(cT[:, c, tok:tok + n_seg], conv[:, c, at - STATE:at - STATE + n_seg],
                                              ACT.Silu, bias=col(C_BCLN, c), scale=col(C_GCLN, c)),
                                "silu" if last else None)
                for n in range(KD):
                    full(sc, "mix", (g, n))
                    ch.step(sc.activation(hT[:, n, 0:n_tok], bank("mix", (g, n))[:, 0:n_tok], ACT.Copy), "delta_t")
                for t in tiles:
                    _, at, rows = TILES[t]
                    sc.wait_ge(sem("x1_squares"), t + 1)
                    root("x1_squares", "rms_x1", t)
                    for hf in range(2):
                        full(sc, "h2T", (t, hf))
                        src = bank("h2T", (t, hf)).rearrange("p (c q) -> p c q", c=4)
                        ch.step(sc.activation(merged[:, 4 * hf:4 * hf + 4, at:at + rows], src[:, :, 0:rows], ACT.Copy), "h2_t")
                for n in range(SEGS):
                    full(sc, "query", (g, n))
                    ch.step(sc.activation(gates[:, n, 0:n_tok], bank("query", (g, n))[:, 0:n_tok], ACT.Copy), "query_t")
                for t in tiles:
                    rows = TILES[t][2]
                    for j in range(4):
                        full(sc, "keyscore", (t, j))
                        ch.go(sc.activation(key_S[t][0:rows, 4 * j:4 * j + 4, :].rearrange("p a b -> p (a b)"),
                                            bank("keyscore", (t, j))[0:rows, :], ACT.Copy), "key_scores")
                if g == 1:
                    for s in range(2):
                        full(sc, "state", s)
                        ch.go(sc.activation(stash[:, s, :], bank("state", s)[0:STATE, :], ACT.Copy), "conv_state")
                for t in (GROUPS[0] if g == 0 else [2]):
                    top_exps(t)

            def gelu_tanh(t):
                sc.wait_ge(sem("gelu_in"), t + 1)
                th = tanh[:, 0:GATHERS[t]]
                ch.go(sc.activation(th, th, ACT.Tanh, scale=GELU_K), "gelu_tanh")

            def copy_h3(t):
                rows = TILES[t][2]
                for hf in range(2):
                    full(sc, "h3T", (t, hf))
                    src = bank("h3T", (t, hf)).rearrange("p (c q) -> p c q", c=4)
                    ch.go(sc.activation(h3T[:, 4 * hf:4 * hf + 4, 0:rows], src[:, :, 0:rows], ACT.Copy), "h3_t")

            def sigmoid(t):
                rows = TILES[t][2]
                for hf in range(2):
                    full(sc, "ple_gate", (t, hf))
                    ch.go(sc.activation(pgate[0:rows, hf * 512:(hf + 1) * 512], bank("ple_gate", (t, hf))[0:rows, :],
                                        ACT.Sigmoid), "ple_gate")

            parts = {"root2": lambda t: root("x2_squares", "rms_x2", t), "h3T_copy": copy_h3, "sigmoid": sigmoid,
                     "root3": lambda t: root("x3_squares", "rms_x3", t)}
            for t in GROUPS[0]:
                gelu_tanh(t)
            sc.wait_ge(sem("key_scores"), 4 * len(TILES))
            for n, (t, j) in enumerate(V_LIST):
                for c, (_, exps, _) in CHOICE.items():
                    if n == exps:
                        top_exps(c)
                last_stage(n, parts)
                if n + GELU_AHEAD - 2 in FIRST[2:5]:
                    gelu_tanh(FIRST.index(n + GELU_AHEAD - 2))
                if j == 0:
                    sc.wait_ge(sem("act"), t + 1)
                if by_vector(t, j):
                    continue
                k = V_ORDINAL[n]
                if k >= DIAGS:
                    sc.wait_ge(v_tensor, k - DIAGS + 1)
                m = ident[:] if t < SAMPLE else fold[:]
                sc.activation(diag[:, k % DIAGS, 0:P if t < SAMPLE else DEC], m, ACT.Copy,
                              scale=dot[:, COLUMN[t] + j:COLUMN[t] + j + 1]).then_inc(sem("diag"), 1)
            for do in parts.values():
                do(SAMPLE)

        @block.vector
        def _(ve):
            ch = Chain(ve, sem("vector_step"))

            def col(base, n=0):
                return cols[:, base + n:base + n + 1]

            def squares(t, src, junk, name):
                rows = TILES[t][2]
                ch.go(ve.tensor_tensor_reduce(junk[0:rows], src, src, 1.0, 0.0, ALU.mult, ALU.add, stat[0:rows, 0:1]), name)

            def normed(t, out, src, gain, rms, ready):
                rows = TILES[t][2]
                ve.wait_ge(sem(rms), t + 1)
                ch.step(ve.reciprocal(stat[0:rows, 2:3], stat[0:rows, 1:2]))
                ch.step(ve.scalar_tensor_tensor(out, src, stat[0:rows, 2:3], gain[0:rows, :], ALU.mult, ALU.mult), ready)

            for buf, value in ((over_d, 1.0 / D), (over_c, 1.0 / DC), (eps, EPS)):
                ve.memset(buf[:], value).then_inc(sem("filled_const"), 1)
            ch.step(ve.memset(glu[:, :, 0:STATE], 0.0))
            ve.wait_ge(loaded["const"], 16 * 8)
            ve.wait_ge(loaded["cache"], 16 * 3)

            def trunk(g):
                n_tok, tiles, cw = WIDTH[g], GROUPS[g], CONVW[g]
                ve.wait_ge(sem("rms_x"), g + 1)
                ch.step(ve.reciprocal(rstd[:, 0:n_tok], tmp[:, 0:n_tok]))
                for c in range(KD):
                    ch.go(ve.scalar_tensor_tensor(hT[:, c, 0:n_tok], hT[:, c, 0:n_tok], col(C_GMIX, c), rstd[:, 0:n_tok],
                                                    ALU.mult, ALU.mult), "h_ready" if c == KD - 1 else None)
                ch.settle()
                yield 4
                if g:
                    ch.step(ve.tensor_copy(glu[:, :, 0:STATE], glu[:, :, 2 * P:2 * P + STATE]))
                    ch.step(ve.tensor_copy(glu[:, :, 2 * P + STATE:2 * P + 2 * STATE], past[:]))
                for c in range(KC):
                    full(ve, "z", (g, c))
                    ve.wait_ge(sem("scalar_z"), len(SCALAR_Z) * g + c + 1)
                    for s, (tok, n_seg, at) in enumerate(SEG[g]):
                        ch.step(ve.scalar_tensor_tensor(glu[:, c, at:at + n_seg], bank("z", (g, c))[:, tok:tok + n_seg],
                                                        col(C_BIN, c), sig[:, c, tok:tok + n_seg], ALU.add, ALU.mult),
                                "glu" if s == len(SEG[g]) - 1 else None)
                    yield 1
                for t in tiles:
                    rows = TILES[t][2]
                    full(ve, "vtok", t)
                    src = bank("vtok", t)
                    if t >= 3:
                        ch.step(ve.tensor_copy(ktok[0:rows, t - 3, :], src[0:rows, P:2 * P]))
                    ch.step(ve.tensor_copy(vtok[0:rows, t if t < SAMPLE else 5, :], src[0:rows, 0:P]), "tokens_v")
                yield 1
                base = KC * TAPS * g
                for w in range(TAPS):
                    for c in range(KC):
                        src, out = glu[:, c, w:w + cw], conv[:, c, 0:cw]
                        tap = col(C_WDW, c * TAPS + w)
                        if w == 0:
                            ve.tensor_scalar(out, src, tap, col(C_BDW, c), ALU.mult, ALU.add).then_inc(sem("conv"), 1)
                        else:
                            ve.wait_ge(sem("conv"), base + KC * (w - 1) + c + 1)
                            ve.scalar_tensor_tensor(out, src, tap, out, ALU.mult, ALU.add).then_inc(sem("conv"), 1)
                    if w % 3 == 2:
                        yield 5
                ve.wait_ge(sem("conv"), base + KC * TAPS)
                for stage, t in attention_order(tiles):
                    rows = TILES[t][2]
                    lo, hi = (P if t == 0 else 0), (2 * P if t < SAMPLE else WINDOW + DEC)
                    S, sm = att_S[t % 2], small[0:rows, t % 2, :]
                    if stage == "s":
                        ve.wait_ge(sem("scores"), PAIRS * (t + 1))
                        for h in range(H):
                            ch.go(ve.scalar_tensor_tensor(S[0:rows, h, lo:hi], dist[0:rows, lo:hi], -SLOPES[h],
                                                          S[0:rows, h, lo:hi], ALU.mult, ALU.add))
                        ch.settle()
                        ch.step(ve.tensor_reduce(sm[:, 8:16], S[0:rows, :, lo:hi], AX, ALU.max))
                        ch.step(ve.tensor_tensor(sm[:, 8:16], sm[:, 8:16], sinks[0:rows, :], ALU.max))
                        ch.go(ve.tensor_tensor(sm[:, 24:32], sinks[0:rows, :], sm[:, 8:16], ALU.subtract))
                        ch.step(ve.tensor_scalar(sm[:, 0:8], sm[:, 8:16], -1.0, None, ALU.mult), "score_max")
                        yield 6
                    if stage == "e":
                        ve.wait_ge(sem("exps"), t + 1)
                        ch.step(ve.tensor_tensor(sm[:, 16:24], sm[:, 16:24], sm[:, 24:32], ALU.add))
                        ch.step(ve.reciprocal(sm[:, 16:24], sm[:, 16:24]))
                        ch.step(ve.tensor_tensor(S[0:rows, :, lo:hi], S[0:rows, :, lo:hi],
                                                 sm[:, 16:24].unsqueeze(2).to_broadcast([rows, H, hi - lo]), ALU.mult), "probs")
                        yield 3
                full(ve, "mean", g)
                for c in range(KC):
                    ch.go(ve.tensor_tensor(conv[:, c, 0:cw], conv[:, c, 0:cw], bank("mean", g)[:, 0:cw], ALU.subtract),
                            "centred" if c == KC - 1 else None)
                yield 2
                ve.wait_ge(sem("rms_conv"), g + 1)
                ch.step(ve.reciprocal(rstd[:, 0:cw], rstd[:, 0:cw]))
                ch.step(ve.tensor_tensor(conv[:, :, 0:cw], conv[:, :, 0:cw],
                                         rstd[:, 0:cw].unsqueeze(1).to_broadcast([P, KC, cw]), ALU.mult), "conv_normed")
                yield 2
                ve.wait_ge(sem("scalar_z"), len(SCALAR_Z) * (g + 1))
                for n in range(KD):
                    full(ve, "attn_out", (g, n))
                    ch.go(ve.scalar_tensor_tensor(merged[:, n, 0:n_tok], bank("conv_out", (g, n))[:, 0:n_tok], col(C_BCOUT, n),
                                                    gates[:, n, 0:n_tok], ALU.add, ALU.mult))
                    ch.step(ve.tensor_tensor(tmp[:, 0:n_tok], bank("attn_out", (g, n))[:, 0:n_tok],
                                             gates[:, KD + n, 0:n_tok], ALU.mult))
                    ch.step(ve.tensor_tensor(merged[:, n, 0:n_tok], merged[:, n, 0:n_tok], tmp[:, 0:n_tok], ALU.add), "merged")
                    yield 1.5
                ve.wait_ge(loaded["x"], 32)
                for t in tiles:
                    rows = TILES[t][2]
                    for hf in range(2):
                        full(ve, "x1", (t, hf))
                        f = slice(hf * 512, (hf + 1) * 512)
                        ch.go(ve.tensor_tensor(x1[0:rows, t, f], bank("x1", (t, hf))[0:rows, :], x1[0:rows, t, f], ALU.add), "x1_ready")
                    ch.settle()
                    squares(t, x1[0:rows, t, :], h2[:, t, :], "x1_squares")
                    yield 3
                    normed(t, h2[0:rows, t, :], x1[0:rows, t, :], g_ffn, "rms_x1", "h2_ready")
                    yield 1.5

            def choice(t):
                rows = TILES[t][2]
                ve.wait_ge(sem("key_scores"), 4 * (t + 1))
                scores = key_S[t][0:rows]
                cand = PT[0:rows].rearrange("p a b -> p (a b)").rearrange("p (r k) -> p r k", r=HEADS)

                def top16(lists):
                    n = len(lists)
                    for values, vals, _ in lists:
                        ch.lag(lambda: ve.max(vals[:, 0:8], values), 1)
                    for values, vals, places in lists:
                        ch.lag(lambda: ve.max_index(places[:, 0:8], vals[:, 0:8], values), n)
                    for values, vals, _ in lists:
                        ch.lag(lambda: ve.match_replace(values, vals[:, 0:8], values, LOWEST), n)
                    for values, vals, _ in lists:
                        ch.lag(lambda: ve.max(vals[:, 8:16], values), n)
                    for values, vals, places in lists:
                        ch.lag(lambda: ve.max_index(places[:, 8:16], vals[:, 8:16], values), n)

                for m in range(0, SEGS, 4):
                    top16([(scores[:, i, :], best[0:rows, i, :], bestid[0:rows, i, :]) for i in range(m, m + 4)])
                    yield 5
                ch.settle()
                ch.go(ve.tensor_copy(bestidf[0:rows], bestid[0:rows]))
                b = best[0:rows].rearrange("p (r two) k -> p r two k", two=2)
                grid = [rows, HEADS, TOPK, TOPK]
                c4 = cand.rearrange("p r (i j) -> p r i j", i=TOPK)
                ch.step(ve.tensor_tensor(c4, b[:, :, 0, :].unsqueeze(3).to_broadcast(grid),
                                         b[:, :, 1, :].unsqueeze(2).to_broadcast(grid), ALU.add))
                yield 2
                for r in range(0, HEADS, 4):
                    top16([(cand[:, i, :], top[0:rows, i, :], pos[0:rows, i, :]) for i in range(r, r + 4)])
                    yield 7
                ch.settle()
                ch.go(ve.tensor_scalar(pos[0:rows, HEADS:2 * HEADS], pos[0:rows, 0:HEADS], 4, None, ALU.logical_shift_right))
                ch.go(ve.tensor_scalar(pos[0:rows, 2 * HEADS:], pos[0:rows, 0:HEADS], TOPK - 1, None, ALU.bitwise_and))
                ch.step(ve.tensor_copy(stat[0:rows, 8:16], top[0:rows, :, 0]))
                ch.go(ve.tensor_copy(posf[0:rows], pos[0:rows, HEADS:]))
                ch.step(ve.tensor_tensor(top[0:rows], top[0:rows], stat[0:rows, 8:16].unsqueeze(2).to_broadcast([rows, HEADS, TOPK]),
                                         ALU.subtract), "top_ready")
                bi = bestidf[0:rows].rearrange("p (r two) k -> p r two k", two=2)
                for side in range(2):
                    places = posf[0:rows, side * HEADS:(side + 1) * HEADS, :].rearrange("p r k -> p (r k)")
                    hot = cand.rearrange("p r (k i) -> p (r k) i", i=TOPK)
                    flat = [rows, PICKS, TOPK]
                    ch.step(ve.tensor_tensor(hot, places.unsqueeze(2).to_broadcast(flat),
                                             iota[0:rows].unsqueeze(1).to_broadcast(flat), ALU.is_equal))
                    yield 2
                    ch.step(ve.tensor_tensor(c4, c4, bi[:, :, side, :].unsqueeze(2).to_broadcast(grid), ALU.mult))
                    yield 2
                    ch.step(ve.tensor_reduce(chosen[0:rows, side, :], hot, AX, ALU.add))
                    yield 2

            def choice_end(t):
                rows = TILES[t][2]
                at = slice(COLUMN[t], COLUMN[t] + PICKS)
                ve.wait_ge(sem("top_exps"), t + 1)
                ch.step(ve.tensor_reduce(stat[0:rows, 16:24], top[0:rows], AX, ALU.add))
                ch.step(ve.reciprocal(stat[0:rows, 16:24], stat[0:rows, 16:24]))
                ch.step(ve.tensor_tensor(gate[0:rows, at].rearrange("p (r k) -> p r k", r=HEADS),
                                         top[0:rows], stat[0:rows, 16:24].unsqueeze(2).to_broadcast([rows, HEADS, TOPK]),
                                         ALU.mult))
                ch.step(ve.scalar_tensor_tensor(expert[0:rows, at], chosen[0:rows, 0, :], float(KEYS),
                                                chosen[0:rows, 1, :], ALU.mult, ALU.add), "experts")

            u_next = [0]

            def dots(n):
                for u in range(u_next[0], u_next[0] + n):
                    t, j = U_LIST[u]
                    if u == FIRST[SAMPLE]:
                        ve.wait_ge(loaded["h2_fold"], 16)
                    ve.wait_ge(u_loaded[u % USLOTS], 16 * (u // USLOTS + 1))
                    row = uring[:, u % USLOTS, :]
                    ve.tensor_tensor_reduce(row, row, h2[:, t, :], 1.0, 0.0, ALU.mult, ALU.add,
                                            dot[:, COLUMN[t] + j:COLUMN[t] + j + 1]).then_inc(u_used, 1)
                u_next[0] += n

            def gelu_in(t):
                at = slice(COLUMN[t], COLUMN[t] + GATHERS[t])
                ve.wait_ge(u_used, FIRST[t + 1])
                if t == SAMPLE:
                    ve.wait_ge(loaded["id_fold"], 32)
                d, th = dot[:, at], tanh[:, 0:GATHERS[t]]
                ch.step(ve.tensor_tensor(th, d, d, ALU.mult))
                ch.step(ve.tensor_scalar(th, th, GELU_C, 1.0, ALU.mult, ALU.add))
                ch.go(ve.scalar_tensor_tensor(gate[:, at], gate[:, at], 0.5, d, ALU.mult, ALU.mult))
                ch.step(ve.tensor_tensor(th, th, d, ALU.mult), "gelu_in")

            def gelu_out(t):
                at = slice(COLUMN[t], COLUMN[t] + GATHERS[t])
                ve.wait_ge(sem("gelu_tanh"), t + 1)
                ch.step(ve.scalar_tensor_tensor(dot[:, at], tanh[:, 0:GATHERS[t]], 1.0, gate[:, at], ALU.add, ALU.mult), "act")

            for _ in trunk(0):
                pass
            for t in GROUPS[0]:
                for _ in choice(t):
                    pass
                choice_end(t)
            due = [0.0]

            def beside(pieces):
                for us in pieces:
                    due[0] = min(due[0] + us * DOTS_PER_US, PHASE1)
                    dots(int(due[0]) - u_next[0])

            beside(trunk(1))
            beside(choice(2))
            choice_end(2)
            dots(PHASE1 - u_next[0])
            for t in GROUPS[0]:
                gelu_in(t)
                gelu_out(t)

            def sum_up(t):
                rows = TILES[t][2]
                ve.wait_ge(v_tensor, len([n for n in V_TENSOR if n < FIRST[t + 1]]))
                ve.wait_ge(v_vector, len([n for n in V_VECTOR if n < FIRST[t + 1]]))
                ch.step(ve.tensor_tensor(x1[0:rows, t, :], acc[t % 2][0:rows, :], x1[0:rows, t, :], ALU.add), "x2_ready")
                ve.wait_ge(loaded["late"], 16 * 5)
                squares(t, x1[0:rows, t, :], h3, "x2_squares")

            def h3_of(t):
                rows = TILES[t][2]
                normed(t, h3[0:rows, :], x1[0:rows, t, :], gains[:, 0, :], "rms_x2", "h3_ready")

            def x3_of(t):
                rows = TILES[t][2]
                for hf in range(2):
                    f = slice(hf * 512, (hf + 1) * 512)
                    ve.wait_ge(sem("ple_gate"), 2 * t + hf + 1)
                    full(ve, "ple", (t, hf))
                    ch.go(ve.tensor_tensor(pgate[0:rows, f], bank("ple", (t, hf))[0:rows, :], pgate[0:rows, f], ALU.mult), "x3_half")
                ch.settle()
                ch.step(ve.tensor_tensor(x1[0:rows, t, :], x1[0:rows, t, :], pgate[0:rows, :], ALU.add))
                squares(t, x1[0:rows, t, :], pgate, "x3_squares")

            def y_of(t):
                rows = TILES[t][2]
                if t >= 2:
                    ve.wait_ge(sem(f"y_stored{t % 2}"), 16 * (t // 2))
                normed(t, y[0:rows, t % 2, :], x1[0:rows, t, :], gains[:, 1, :], "rms_x3", "y_ready")

            parts = {"sum": sum_up, "h3": h3_of, "x3": x3_of, "y": y_of}
            choosing = {t: choice(t) for t in CHOICE}
            for n, (t, j) in enumerate(V_LIST):
                if n + GELU_AHEAD in FIRST[2:5]:
                    gelu_in(FIRST.index(n + GELU_AHEAD))
                if n + GELU_AHEAD - 4 in FIRST[2:5]:
                    gelu_out(FIRST.index(n + GELU_AHEAD - 4))
                for c, (begin, _, end) in CHOICE.items():
                    if begin <= n < end and (n - begin) % CHOICE_STRIDE == 0:
                        next(choosing[c], None)
                    if n == end:
                        choice_end(c)
                last_stage(n, parts)
                if PHASE1 + n < len(U_LIST):
                    dots(1)
                if by_vector(t, j):
                    k = V_ORDINAL[n]
                    ve.wait_ge(v_loaded[n % VSLOTS], 16 * (n // VSLOTS + 1))
                    if k:
                        ve.wait_ge(v_vector, k)
                    ve.scalar_tensor_tensor(x1[:, t, :], vring[:, n % VSLOTS, :], dot[:, COLUMN[t] + j:COLUMN[t] + j + 1],
                                            x1[:, t, :], ALU.mult, ALU.add).then_inc(v_vector, 1)
            for do in parts.values():
                do(SAMPLE)

        @block.gpsimd
        def _(po):
            def gather_u(n):
                t, j = U_LIST[n]
                if j == 0:
                    po.wait_ge(sem("experts"), t + 1)
                    if t == SAMPLE:
                        po.wait_ge(loaded["id_fold"], 32)
                if n >= USLOTS:
                    po.wait_ge(u_used, n - USLOTS + 1)
                c = COLUMN[t] + j
                po.indirect_dma_start(uring[:, n % USLOTS, :], None, a["expert_u"],
                                      bass.IndirectOffsetOnAxis(ap=expert[:, c:c + 1], axis=0)).then_inc(u_loaded[n % USLOTS], 16)

            def gather_v(n):
                t, j = V_LIST[n]
                if n >= VSLOTS:
                    m = n - VSLOTS
                    po.wait_ge(v_vector if by_vector(*V_LIST[m]) else v_tensor, V_ORDINAL[m] + 1)
                c = COLUMN[t] + j
                po.indirect_dma_start(vring[:, n % VSLOTS, :], None, a["expert_v"],
                                      bass.IndirectOffsetOnAxis(ap=expert[:, c:c + 1], axis=0)).then_inc(v_loaded[n % VSLOTS], 16)

            for n in range(PHASE1):
                gather_u(n)
            po.wait_ge(sem("key_scores"), 4 * len(TILES))
            for n in range(BEATS):
                gather_v(n)
                if PHASE1 + n < len(U_LIST):
                    gather_u(PHASE1 + n)


_OUTS = {"y_p": (SEQ, D), "y_s": (DEC, D), "nk_p": (WINDOW, KV * HD), "nv_p": (WINDOW, KV * HD), "nc_p": (STATE, DC),
         "nk_s": (WINDOW, KV * HD), "nv_s": (WINDOW, KV * HD), "nc_s": (STATE, DC)}


def _blocks(w, n, k):
    return np.ascontiguousarray(w.reshape(k, P, n, P).transpose(2, 1, 0, 3))


def _rows(w, k):
    return np.ascontiguousarray(w.reshape(k, P, -1).transpose(1, 0, 2))


def _column(v):
    return v.reshape(-1, P).T


def layout(i):
    i = {k: np.asarray(v) for k, v in i.items()}
    x = np.concatenate([i["x_prompt"][0], i["x_sample"][0]])
    pe = np.concatenate([i["p_prompt"][0, 0], i["p_sample"][0, 0]])
    heads = np.arange(H * HD).reshape(KV, PAIRS, HD).transpose(1, 0, 2).reshape(-1)
    order = np.arange(NZ * P)
    order[Q0 * P:K0 * P] = Q0 * P + heads
    w_in, b_in = i["w_in"][0][:, order], i["b_in"][0][order]
    w_br = np.concatenate([i["w_cout"][0], i["w_aout"][0][heads]])
    q, k = np.arange(P)[:, None], np.arange(2 * P)[None, :]
    first = q // CHUNK * CHUNK
    seen = (k >= first) & (k < first + WINDOW + CHUNK)
    dist = np.where(seen, np.abs(q + WINDOW - k), 1e32).astype(np.float32)
    cols = np.concatenate([
        _column(b_in), _column(i["g_mix"][0]), _column(i["b_dw"][0]), _column(i["g_cln"][0]), _column(i["b_cln"][0]),
        _column(i["b_cout"][0]), i["w_dw"][0].reshape(TAPS, KC, P).transpose(2, 1, 0).reshape(P, -1)], axis=1)
    keys = np.stack([i["sub_keys1"][0], i["sub_keys2"][0]])
    return {
        "x_t": _rows(x.T, KD), "x_p": i["x_prompt"][0], "x_s": i["x_sample"][0], "p_t": _rows(pe.T, KP),
        "cols": cols, "ident": np.eye(P, dtype=np.float32), "fold": np.tile(np.eye(DEC, dtype=np.float32), (2, 1)), "dist": dist,
        "iota": np.tile(np.arange(TOPK, dtype=np.float32), (P, 1)), "keys_t": keys.transpose(2, 0, 1),
        "sinks": i["sinks"], "g_ffn": i["g_ffn"], "g_ple": i["g_ple"], "g_final": i["g_final"][None],
        "cache_kt": i["cache_k"].reshape(WINDOW, P).T, "cache_k": i["cache_k"].reshape(WINDOW, P),
        "cache_v": i["cache_v"].reshape(WINDOW, P), "past_t": _rows(i["state_conv"][0, 0].T, KC),
        "w_in": _blocks(w_in, NZ, KD), "w_br": _blocks(w_br, KD, KD), "w_out": _blocks(i["w_out"][0], KD, KD),
        "w_query": _blocks(i["w_query"][0], SEGS, KD), "w_ple": _rows(i["w_ple"][0], KP), "w_pg": _rows(i["w_ple_gate"][0], KD),
        "expert_u": i["expert_u"][0], "expert_v": i["expert_v"][0],
    }


def kernel(**inputs):
    import concourse.bacc as bacc
    from concourse.bass_utils import run_bass_kernel_spmd

    arrays = {k: np.ascontiguousarray(v) for k, v in layout(inputs).items()}
    nc = bacc.Bacc("TRN2", target_bir_lowering=False, num_devices=1)
    a = {k: nc.dram_tensor(k, v.shape, F32, kind="ExternalInput").ap() for k, v in arrays.items()}
    a |= {k: nc.dram_tensor(k, s, F32, kind="ExternalOutput").ap() for k, s in _OUTS.items()}
    build(nc, a)
    r = run_bass_kernel_spmd(nc, [arrays], core_ids=[0]).results[0]
    kv = (1, 1, WINDOW, KV, HD)
    return (r["y_p"].reshape(1, SEQ, D), r["y_s"].reshape(1, DEC, D), r["nk_p"].reshape(kv), r["nv_p"].reshape(kv),
            r["nc_p"].reshape(1, 1, STATE, DC), r["nk_s"].reshape(kv), r["nv_s"].reshape(kv),
            r["nc_s"].reshape(1, 1, STATE, DC))
```

```python
from contextlib import ExitStack

import numpy as np

import concourse.bass as bass
from concourse import mybir

F32 = mybir.dt.float32
U32 = mybir.dt.uint32
ALU = mybir.AluOpType
ACT = mybir.ActivationFunctionType
AX = mybir.AxisListType.X

P = 128
D, DC, DP = 1024, 512, 256
KD, KC, KP = D // P, DC // P, DP // P
SEQ, DEC = 512, 64
TOK = SEQ + DEC
H, KV, HD = 8, 2, 64
PAIRS = H // KV
CHUNK, WINDOW = 64, 128
TAPS = 31
STATE = TAPS - 1
NZ = (2 * DC + H * HD + 2 * KV * HD + 2 * D) // P
HEADS, TOPK, KEYS = 8, 16, 128
SEGS = 2 * HEADS
PICKS = HEADS * TOPK
EPS = 1e-6
SLOPES = [2.0 ** (-8.0 * (h + 1) / H) for h in range(H)]
GELU_C, GELU_K = 0.044715, 0.7978845608028654
LOWEST = -3.0e38

TILES = [(0, 0, P), (0, P, P), (1, 0, P), (1, P, P), (1, 2 * P, DEC)]
GROUPS = [[t for t in range(len(TILES)) if TILES[t][0] == g] for g in range(2)]
WIDTH = [sum(TILES[t][2] for t in GROUPS[g]) for g in range(2)]
WMAX = max(WIDTH)
START = [0, WIDTH[0]]
SAMPLE = len(TILES) - 1
PASSES = [[[0], [1]], [[2, 3, 4]]]
Q0, K0, V0, G0 = 2 * KC, 2 * KC + 4, 2 * KC + 5, 2 * KC + 6
ZORDER = [n for c in range(KC) for n in (KC + c, c)] + [K0, V0] + list(range(Q0, K0)) + list(range(G0, NZ))
SCALAR_Z = [n for n in ZORDER if n >= KC]
SEG = [[(0, 2 * P, STATE)], [(0, 2 * P, STATE), (2 * P, DEC, 2 * STATE + 2 * P)]]
CONVW = [2 * P, 2 * P + STATE + DEC]
GLUW = 2 * STATE + 2 * P + DEC
KCOLS = WINDOW + SEQ + WINDOW + DEC

BANKS = 4
WSLOTS = 4
USLOTS = 6
VSLOTS = 9
CONV_BLOCKS = [KC, KC - 1]
DIAGS = 8
ARENA = 32672
GATHERS = [PICKS] * 4 + [PICKS // 2]
COLUMN = [t * PICKS for t in range(5)]
U_LIST = [(t, j) for t in range(5) for j in range(GATHERS[t])]
V_LIST = [(t, j) for t in range(5) for j in range(GATHERS[t])]
PHASE1 = GATHERS[0] + 34
BEATS = len(V_LIST)
FIRST = [sum(GATHERS[:t]) for t in range(6)]


def by_vector(t, j):
    return j % (3 if t < SAMPLE else 2) == 1


V_VECTOR = [n for n, (t, j) in enumerate(V_LIST) if by_vector(t, j)]
V_TENSOR = [n for n, (t, j) in enumerate(V_LIST) if not by_vector(t, j)]
SAMPLE_VECTOR = len([n for n in V_VECTOR if n < BEATS - GATHERS[SAMPLE]])
V_ORDINAL = {n: k for part in (V_VECTOR, V_TENSOR) for k, n in enumerate(part)}

U_BY = []
for n in range(BEATS):
    u = U_BY[-1] if U_BY else PHASE1
    U_BY.append(min(u + (1 if u < FIRST[4] else n % 2), len(U_LIST)))

HOOKS = {"sum": 4, "root2": 7, "h3": 9, "h3T": 11, "h3T_copy": 13, "ple_0": 18, "ple_1": 30, "sigmoid": 38, "x3": 41, "root3": 43,
         "y": 45}
FIRST_LATER = 72
CHOICE = {2: (0, 56, 58), 3: (60, 116, 118), 4: (120, 176, 178)}
CHOICE_STRIDE = 4
GELU_AHEAD = 16
assert all(U_BY[FIRST[t] - GELU_AHEAD - 1] >= FIRST[t + 1] for t in range(1, len(TILES)))


DOTS = {"choice_end": 5, "h": 5, "glu": 6, "conv": (8, 6, 4, 6, 8, 8), "mean": 6, "norm": 6, "merged": 2, "mix": 3, "choice": 5}


def hook(t, part):
    return FIRST[t + 1] + HOOKS[part] + (FIRST_LATER if t == 0 and part != "sum" else 0)


def inner_stages(g):
    a, b, *c = GROUPS[g]
    mix = [("z", n) for n in range(G0, NZ)]

    def dots(n):
        return [("dots", n)] if g else []

    out = [("tap_diags", KC - 1)] * g
    for k in range(KC):
        out += [("z", KC + k), ("z", k), ("glu", k)] + dots(DOTS["glu"])
    cuts = (0, 6, 9, 14, 19, 25, TAPS) if g else (0, 8, 12, 16, 22, 27, TAPS)
    conv = [[("conv", taps)] + dots(n) for taps, n in zip(zip(cuts, cuts[1:]), DOTS["conv"])]
    out += conv[0] + [("z", n) for n in (K0, V0, *range(Q0, K0))] + [("vtok", t) for t in GROUPS[g]] + [("s", a), ("s", b)]
    by_tensor = [KC - 1] * g
    out += conv[1] + mix[0:2] + [("e", a)] + conv[2] + mix[2:4] + [("e", b)] + mix[4:6] + conv[3]
    out += [("p", a)] + [("s", t) for t in c] + mix[6:8] + conv[4] + [("p", b)]
    out += [("conv_tensor", n) for n in by_tensor] + [("e", t) for t in c] + mix[8:9] + [("conv_drain", n) for n in by_tensor]
    out += mix[9:10] + conv[5] + [("p", t) for t in c] + mix[10:11]
    out += [("mean", 0)] + dots(DOTS["mean"]) + mix[11:12] + [("square", 0)] + mix[12:13] + [("var", 0)] + mix[13:]
    return out + [("norm", 0)] + dots(DOTS["norm"])


C_BIN, C_GMIX, C_BDW, C_GCLN, C_BCLN, C_BCOUT, C_WDW = 0, 30, 38, 42, 46, 50, 58
NCOLS = C_WDW + KC * TAPS


def peer_order(part):
    out = []
    for n in range(SEGS):
        out.append(("query", n))
        if len(part) == 1 and n > 4 and n % 4 == 1:
            out.append(("keyscore", (part[0], n // 4 - 1)))
    return out + [("keyscore", (t, j)) for t in part for j in range(3 if len(part) == 1 else 0, 4)]


def plan_units():
    units, count = [], {}

    def unit(name, key, sem, step=1):
        count[sem] = count.get(sem, 0) + step
        units.append((name, key, sem, count[sem]))

    for g in range(2):
        unit("ms", g, "rms_x")
        for stage, k in inner_stages(g):
            if stage == "z":
                unit("z", (g, k), "scalar_z" if k >= KC else "glu")
            if stage == "vtok":
                unit("vtok", k, "tokens_v")
            if stage == "s":
                for j in range(PAIRS):
                    unit("score", (k, j), "scores")
            if stage == "p":
                for j in range(PAIRS):
                    unit("probT", (k, j), "probs_t")
                unit("attT", k, "att_t")
            if stage == "conv_tensor":
                unit("conv", k, "conv_tensor")
            if stage == "mean":
                unit("mean", g, "centred")
            if stage == "var":
                unit("var", g, "rms_conv")
        for n in range(KD):
            unit("conv_out", (g, n), "merged", 1)
            unit("attn_out", (g, n), "merged", 0)
        for n in range(KD):
            unit("mix", (g, n), "delta_t")
        for t in GROUPS[g]:
            for hf in range(2):
                unit("x1", (t, hf), "x1_ready")
        for part in PASSES[g]:
            for t in part:
                for hf in range(2):
                    unit("h2T", (t, hf), "h2_t")
            for what, k in peer_order(part):
                if what == "query":
                    unit("query", (part[0], k), "query_t")
                else:
                    unit("keyscore", k, "key_scores")
        if g == 1:
            for s in range(2):
                unit("state", s, "conv_state")
    for t in range(len(TILES)):
        for hf in range(2):
            unit("h3T", (t, hf), "h3_t")
        for hf in range(2):
            unit("ple_gate", (t, hf), "ple_gate")
            unit("ple", (t, hf), "x3_half")
    return units


UNITS = plan_units()
AT = {(name, key): u for u, (name, key, _, _) in enumerate(UNITS)}
WEIGHTS = [
    (what, n, AT[unit, (key, n)])
    for g in range(2)
    for what, unit, order, key in [("w_in", "z", ZORDER, g), ("w_br", "attn_out", range(KD), g), ("w_out", "mix", range(KD), g)]
    + [("w_query", "query", range(SEGS), part[0]) for part in PASSES[g]]
    for n in order
]
SECOND_GROUP = NZ + 2 * KD + len(PASSES[0]) * SEGS


def build(nc, a):
    ctx = ExitStack()

    def sb(name, shape, dt=F32):
        return ctx.enter_context(nc.sbuf_tensor(f"{name}_buf", shape, dt))

    with ctx:
        cols = sb("cols", [P, NCOLS])
        g_ffn = sb("g_ffn", [P, D])
        ident = sb("ident", [P, P])
        fold = sb("fold", [P, DEC])
        sinks = sb("sinks", [P, H])
        iota = sb("iota", [P, TOPK])
        keys_t = sb("keys_t", [P, 2, KEYS])
        eps = sb("eps", [P, 1])
        x1 = sb("x1", [P, len(TILES), D])
        h2 = sb("h2", [P, len(TILES), D])
        expert = sb("expert", [P, len(TILES) * PICKS], U32)
        gate = sb("gate", [P, len(TILES) * PICKS])
        dot = sb("dot", [P, len(TILES) * PICKS])
        tanh = sb("tanh", [P, PICKS])
        tap_diag = [h2[:, 2 + w // KD, w % KD * P:(w % KD + 1) * P] for w in range(3 * KD)]
        tap_diag += [table[:, (2 + k) * PICKS:(3 + k) * PICKS] for table in (gate, dot) for k in range(3)] + [tanh[:]]
        assert len(tap_diag) == TAPS and PICKS == P
        small = sb("small", [P, 2, 32])
        stat = sb("stat", [P, 48])
        uring = sb("uring", [P, USLOTS, D])

        arena = sb("arena", [P, ARENA])
        used = [0]

        def take(*shape, dt=F32, at=None):
            n = int(np.prod(shape))
            if at is not None:
                used[0] = at
            view = arena[:, used[0]:used[0] + n]
            used[0] += n
            assert used[0] <= ARENA, used[0]
            if dt != F32:
                view = view.bitcast(dt)
            names = "abcd"[:len(shape)]
            return view.rearrange(f"p ({' '.join(names)}) -> p {' '.join(names)}", **dict(zip(names, shape))) if len(shape) > 1 else view

        wring = take(WSLOTS, KD, P, at=0)
        gates = take(SEGS, WMAX)
        rstd = take(GLUW)
        over_d = take(P)
        over_c = take(P)
        dist = take(2 * P)
        used[0] = late = VSLOTS * D + DIAGS * P
        sig = take(KC, WMAX)
        qT = take(PAIRS, WMAX)
        kT = take(KCOLS)
        vT = take(WMAX)
        tmp = take(WMAX)
        vtok = take(6, P)
        ktok = take(2, P)
        glu = take(KC, GLUW)
        conv = take(KC, CONVW[1])
        past = take(KC, STATE)
        attT = take(PAIRS, WMAX)
        hT = take(KD, WMAX)
        merged = take(KD, WMAX)
        hT_at, merged_at = used[0] - 2 * KD * WMAX, used[0] - KD * WMAX
        S0 = take(H * 2 * P)
        PT = take(H * 2, P)
        best = take(SEGS, TOPK)
        bestid = take(SEGS, TOPK, dt=U32)
        bestidf = take(SEGS, TOPK)
        top = take(HEADS, TOPK)
        pos = take(3 * HEADS, TOPK, dt=U32)
        posf = take(2 * HEADS, TOPK)
        chosen = take(2, PICKS)
        S3 = take(H * 2 * P)
        S1 = take(H * 2 * P, at=hT_at)
        S2 = take(H * 2 * P, at=merged_at)
        convsq = take(KC, CONVW[1], at=merged_at)
        stash = sig.rearrange("p a b -> p (a b)")[0:STATE, 0:2 * DC].rearrange("p (s c) -> p s c", s=2)
        cT = sig
        att_S = [b.rearrange("p (h s) -> p h s", h=H) for b in (S0, S2)]
        key_S = {t: b.rearrange("p (m k) -> p m k", k=KEYS) for t, b in zip(range(5), (S0, S3, S0, S1, S2))}
        vring = take(VSLOTS, D, at=0)
        diag = take(DIAGS, P)
        assert used[0] <= late
        w_pg = take(KD, D, at=late)
        w_ple = take(KP, D)
        p_t = take(KP, TOK)
        gains = take(2, D)
        h3 = take(D)
        h3T = take(KD, P)
        pgate = take(D)
        y = take(2, D)

        ring = [ctx.enter_context(nc.psum_tensor(f"ring{b}", [P, 512], F32)) for b in range(BANKS)]
        acc = [ctx.enter_context(nc.psum_tensor(f"acc{b}", [P, D], F32)) for b in range(2)]

        sems = {}

        def sem(name):
            if name not in sems:
                sems[name] = ctx.enter_context(nc.semaphore(name))
            return sems[name]

        filled = sem("filled")
        loaded = {k: sem(f"loaded_{k}") for k in ("const", "xT0", "xT1", "x", "late", "cache", "h2_fold", "id_fold")}
        w_loaded = [sem(f"w_loaded{i}") for i in range(WSLOTS)]
        u_loaded = [sem(f"u_loaded{i}") for i in range(USLOTS)]
        v_loaded = [sem(f"v_loaded{i}") for i in range(VSLOTS)]
        u_used, v_tensor, v_vector = sem("u_used"), sem("v_tensor"), sem("v_vector")
        stored = sem("stored")

        block = ctx.enter_context(nc.Block())

        def bank(name, key):
            return ring[AT[name, key] % BANKS]

        def full(eng, name, key):
            eng.wait_ge(filled, AT[name, key] + 1)

        class Chain:

            def __init__(self, eng, own):
                self.eng, self.own, self.count, self.last = eng, own, {}, None

            def go(self, ins, name=None):
                s = sem(name) if name else self.own
                self.count[s] = self.count.get(s, 0) + 1
                ins.then_inc(s, 1)
                self.last = s

            def settle(self):
                self.eng.wait_ge(self.last, self.count[self.last])

            def step(self, ins, name=None):
                self.go(ins, name)
                self.settle()

            def lag(self, make, n):
                c = self.count.get(self.own, 0)
                if c - n + 1 > 0:
                    self.eng.wait_ge(self.own, c - n + 1)
                self.go(make())

        side = uring[:, 0, :]

        def last_stage(n, parts):
            for t in range(SAMPLE):
                for part, do in parts.items():
                    if n == hook(t, part):
                        do(t)

        @block.sync
        def _(sp):
            sp.dma_start(hT[:, :, 0:WIDTH[0]], a["x_t"][:, :, 0:WIDTH[0]]).then_inc(loaded["xT0"], 16)
            for name, to in (("cols", cols[:]), ("ident", ident[:]), ("dist", dist), ("iota", iota[:]), ("keys_t", keys_t[:])):
                sp.dma_start(to, a[name]).then_inc(loaded["const"], 16)
            sp.dma_start(sinks[:], a["sinks"].to_broadcast([P, H])).then_inc(loaded["const"], 16)
            sp.dma_start(fold[:], a["fold"]).then_inc(loaded["const"], 16)
            sp.dma_start(g_ffn[:], a["g_ffn"].to_broadcast([P, D])).then_inc(loaded["const"], 16)
            sp.dma_start(kT[:, WINDOW + SEQ:2 * WINDOW + SEQ], a["cache_kt"]).then_inc(loaded["cache"], 16)
            sp.dma_start(vtok[:, 4, :], a["cache_v"]).then_inc(loaded["cache"], 16)
            sp.dma_start(past[:], a["past_t"]).then_inc(loaded["cache"], 16)

            def extra(i):
                if i == 8:
                    sp.dma_start(x1[:, 0:4, :], a["x_p"].rearrange("(t p) d -> p t d", p=P)).then_inc(loaded["x"], 16)
                    sp.dma_start(x1[0:DEC, 4, :], a["x_s"]).then_inc(loaded["x"], 16)
                    sp.dma_start(a["nk_s"][0:DEC, :], a["cache_k"][DEC:WINDOW, :]).then_inc(stored, 16)
                    sp.dma_start(a["nv_s"][0:DEC, :], a["cache_v"][DEC:WINDOW, :]).then_inc(stored, 16)
                if i == SECOND_GROUP:
                    full(sp, "x1", (GROUPS[0][-1], 1))
                    sp.dma_start(hT[:, :, 0:WIDTH[1]], a["x_t"][:, :, WIDTH[0]:TOK]).then_inc(loaded["xT1"], 16)

            for i, (what, n, _) in enumerate(WEIGHTS):
                extra(i)
                if i >= WSLOTS:
                    sp.wait_ge(filled, WEIGHTS[i - WSLOTS][2] + 1)
                sp.dma_start(wring[:, i % WSLOTS], a[what][n]).then_inc(w_loaded[i % WSLOTS], 16)
            sp.wait_ge(sem("tokens_v"), 5)
            for t, rows, nk, nv, at in ((3, P, "nk_p", "nv_p", 0), (4, DEC, "nk_s", "nv_s", DEC)):
                sp.dma_start(a[nk][at:at + rows, :], ktok[0:rows, t - 3, :]).then_inc(stored, 16)
                sp.dma_start(a[nv][at:at + rows, :], vtok[0:rows, 3 if t == 3 else 5, :]).then_inc(stored, 16)
            sp.wait_ge(sem("conv_state"), 2)
            for s, name in enumerate(("nc_p", "nc_s")):
                sp.dma_start(a[name], stash[:, s, :]).then_inc(stored, 16)
            sp.wait_ge(sem("h2_ready"), len(TILES))
            sp.dma_start(h2[DEC:P, SAMPLE, :], h2[0:DEC, SAMPLE, :]).then_inc(loaded["h2_fold"], 16)
            sp.wait_ge(sem("experts"), len(TILES))
            sp.wait_ge(sem("expert_weights"), len(TILES))
            sp.wait_ge(stored, 16 * 8)
            c = COLUMN[SAMPLE]
            for table in (expert, gate):
                sp.dma_start(table[DEC:P, c:c + PICKS // 2], table[0:DEC, c + PICKS // 2:c + PICKS]).then_inc(loaded["id_fold"], 16)
            for name, to in (("w_pg", w_pg), ("w_ple", w_ple), ("p_t", p_t)):
                sp.dma_start(to, a[name]).then_inc(loaded["late"], 16)
            for i, name in enumerate(("g_ple", "g_final")):
                sp.dma_start(gains[:, i, :], a[name].to_broadcast([P, D])).then_inc(loaded["late"], 16)
            for t, (g, at, rows) in enumerate(TILES):
                sp.wait_ge(sem("y_ready"), t + 1)
                to = a["y_p"][t * P:(t + 1) * P, :] if t < 4 else a["y_s"]
                sp.dma_start(to, y[0:rows, t % 2, :]).then_inc(sem(f"y_stored{t % 2}"), 16)
            sp.wait_ge(sem("y_stored0"), 16 * 3)
            sp.wait_ge(sem("y_stored1"), 16 * 2)

        @block.tensor
        def _(pe):
            wi = [0]

            def begin(name, key):
                u = AT[name, key]
                if u >= BANKS:
                    pe.wait_ge(sem(UNITS[u - BANKS][2]), UNITS[u - BANKS][3])
                return ring[u % BANKS]

            def weights():
                i = wi[0]
                wi[0] += 1
                pe.wait_ge(w_loaded[i % WSLOTS], 16 * (i // WSLOTS + 1))
                return wring[:, i % WSLOTS]

            def product(out, w, x, ks, last=None):
                for c in range(ks):
                    ins = pe.matmul(out, w(c), x(c), start=(c == 0), stop=(c == ks - 1))
                return ins

            pe.wait_ge(loaded["const"], 16 * 8)
            pe.wait_ge(loaded["cache"], 16 * 3)
            pe.wait_ge(sem("filled_const"), 3)
            for g in range(2):
                n_tok, tiles, cw = WIDTH[g], GROUPS[g], CONVW[g]
                pe.wait_ge(sem("x_squared"), g + 1)
                out = begin("ms", g)
                product(out[:, 0:n_tok], lambda c: over_d, lambda c: merged[:, c, 0:n_tok], KD).then_inc(filled, 1)
                pe.wait_ge(sem("h_ready"), g + 1)
                for stage, k in inner_stages(g):
                    if stage == "z":
                        out, w = begin("z", (g, k)), weights()
                        product(out[:, 0:n_tok], lambda c: w[:, c, :], lambda c: hT[:, c, 0:n_tok], KD).then_inc(filled, 1)
                    if stage == "vtok":
                        t = k
                        if t == tiles[0]:
                            pe.wait_ge(sem("scalar_z"), len(SCALAR_Z) * g + SCALAR_Z.index(V0) + 1)
                        _, at, rows = TILES[t]
                        kat = WINDOW + t * P if t < SAMPLE else KCOLS - DEC
                        out = begin("vtok", t)
                        pe.transpose(out[0:rows, 0:P], vT[:, at:at + rows], ident[:])
                        pe.transpose(out[0:rows, P:2 * P], kT[:, kat:kat + rows], ident[:]).then_inc(filled, 1)
                    if stage in ("s", "p"):
                        t = k
                        _, at, rows = TILES[t]
                        lo, hi = (P if t == 0 else 0), (2 * P if t < SAMPLE else WINDOW + DEC)
                        band = t * P if t < SAMPLE else WINDOW + SEQ
                        S = att_S[t % 2]
                    if stage == "s":
                        if t == tiles[0]:
                            pe.wait_ge(sem("scalar_z"), len(SCALAR_Z) * g + SCALAR_Z.index(K0 - 1) + 1)
                        for j in range(PAIRS):
                            out = begin("score", (t, j))
                            f = slice(j // 2 * HD, (j // 2 + 1) * HD)
                            for b in range(2):
                                ins = pe.matmul(out[0:rows, b * 2 * P + lo:b * 2 * P + hi], qT[f, j % 2 * 2 + b, at:at + rows],
                                                kT[f, band + lo:band + hi], start=True, stop=True)
                            ins.then_inc(filled, 1)
                    if stage == "p":
                        pe.wait_ge(sem("probs"), t + 1)
                        for j in range(PAIRS):
                            out = begin("probT", (t, j))
                            for kv in range(KV):
                                for part in range(lo // P, 2):
                                    a0, a1 = part * P, min((part + 1) * P, hi)
                                    b = (2 * kv + part) * P
                                    ins = pe.transpose(out[0:a1 - a0, b:b + rows], S[0:rows, PAIRS * kv + j, a0:a1],
                                                       ident[0:rows, 0:rows])
                            ins.then_inc(filled, 1)
                        pe.wait_ge(sem("probs_t"), PAIRS * (t + 1))
                        pe.wait_ge(sem("tokens_v"), t + 1)
                        out = begin("attT", t)
                        for j in range(PAIRS):
                            for kv in range(KV):
                                for part in range(lo // P, 2):
                                    n_k = min((part + 1) * P, hi) - part * P
                                    vt = t - 1 + part if t < SAMPLE else 4 + part
                                    ins = pe.matmul(out[kv * HD:(kv + 1) * HD, j * P:j * P + rows],
                                                    vtok[0:n_k, vt, kv * HD:(kv + 1) * HD],
                                                    PT[0:n_k, 4 * j + 2 * kv + part, 0:rows],
                                                    start=(part == lo // P), stop=(part == 1))
                        ins.then_inc(filled, 1)
                    if stage == "conv_tensor":
                        pe.wait_ge(sem("glu"), 2 * KC)
                        pe.wait_ge(sem("tap_diags"), TAPS)
                        out = begin("conv", k)
                        product(out[:, 0:cw], lambda w: tap_diag[w], lambda w: glu[:, k, w:w + cw], TAPS).then_inc(filled, 1)
                    if stage == "mean":
                        pe.wait_ge(sem("conv"), TAPS * sum(CONV_BLOCKS[0:g + 1]))
                        if g:
                            pe.wait_ge(sem("conv_tensor"), 1)
                        out = begin("mean", g)
                        product(out[:, 0:cw], lambda c: over_c, lambda c: conv[:, c, 0:cw], KC).then_inc(filled, 1)
                    if stage == "var":
                        pe.wait_ge(sem("conv_squared"), g + 1)
                        out = begin("var", g)
                        product(out[:, 0:cw], lambda c: over_c, lambda c: convsq[:, c, 0:cw], KC).then_inc(filled, 1)
                pe.wait_ge(sem("silu"), g + 1)
                pe.wait_ge(sem("att_t"), tiles[-1] + 1)
                for n in range(KD):
                    out, w = begin("conv_out", (g, n)), weights()
                    product(out[:, 0:n_tok], lambda c: w[:, c, :], lambda c: cT[:, c, 0:n_tok], KC).then_inc(filled, 1)
                    out = begin("attn_out", (g, n))
                    product(out[:, 0:n_tok], lambda c: w[:, KC + c, :], lambda c: attT[:, c, 0:n_tok], KC).then_inc(filled, 1)
                pe.wait_ge(sem("merged"), KD * (g + 1))
                for n in range(KD):
                    out, w = begin("mix", (g, n)), weights()
                    product(out[:, 0:n_tok], lambda c: w[:, c, :], lambda c: merged[:, c, 0:n_tok], KD).then_inc(filled, 1)
                pe.wait_ge(sem("delta_t"), KD * (g + 1))
                for t in tiles:
                    _, at, rows = TILES[t]
                    for hf in range(2):
                        out = begin("x1", (t, hf))
                        for c in range(4):
                            ins = pe.transpose(out[0:rows, c * P:(c + 1) * P], hT[:, 4 * hf + c, at:at + rows], ident[:])
                        ins.then_inc(filled, 1)
                for part in PASSES[g]:
                    for t in part:
                        _, at, rows = TILES[t]
                        pe.wait_ge(sem("h2_ready"), t + 1)
                        for hf in range(2):
                            out = begin("h2T", (t, hf))
                            for c in range(4):
                                f = (4 * hf + c) * P
                                ins = pe.transpose(out[:, c * P:c * P + rows], h2[0:rows, t, f:f + P], ident[0:rows, 0:rows])
                            ins.then_inc(filled, 1)
                    pe.wait_ge(sem("h2_t"), 2 * (part[-1] + 1))
                    lo, hi = TILES[part[0]][1], TILES[part[-1]][1] + TILES[part[-1]][2]
                    done = SEGS * (PASSES[0] + PASSES[1]).index(part)
                    for what, k in peer_order(part):
                        if what == "query":
                            out, w = begin("query", (part[0], k)), weights()
                            product(out[:, 0:hi - lo], lambda c: w[:, c, :], lambda c: merged[:, c, lo:hi], KD).then_inc(filled, 1)
                        else:
                            t, j = k
                            _, at, rows = TILES[t]
                            pe.wait_ge(sem("query_t"), done + 4 * j + 4)
                            out = begin("keyscore", (t, j))
                            for i in range(4):
                                m = 4 * j + i
                                ins = pe.matmul(out[0:rows, i * P:(i + 1) * P], gates[:, m, at:at + rows],
                                                keys_t[:, m % 2, :], start=True, stop=True)
                            ins.then_inc(filled, 1)
                if g == 1:
                    for s in range(2):
                        _, n_seg, at = SEG[1][s]
                        at += n_seg - STATE
                        out = begin("state", s)
                        for c in range(KC):
                            ins = pe.transpose(out[0:STATE, c * P:(c + 1) * P], glu[:, c, at:at + STATE], ident[:])
                        ins.then_inc(filled, 1)

            def turn_h3(t):
                rows = TILES[t][2]
                pe.wait_ge(sem("h3_ready"), t + 1)
                for hf in range(2):
                    out = begin("h3T", (t, hf))
                    for c in range(4):
                        f = (4 * hf + c) * P
                        ins = pe.transpose(out[:, c * P:c * P + rows], h3[0:rows, f:f + P], ident[0:rows, 0:rows])
                    ins.then_inc(filled, 1)

            def ple(t, hf):
                _, at, rows = TILES[t]
                pe.wait_ge(loaded["late"], 16 * 5)
                pe.wait_ge(sem("h3_t"), 2 * (t + 1))
                tok = START[TILES[t][0]] + at
                f = slice(hf * 512, (hf + 1) * 512)
                out = begin("ple_gate", (t, hf))
                product(out[0:rows, :], lambda c: h3T[:, c, 0:rows], lambda c: w_pg[:, c, f], KD).then_inc(filled, 1)
                out = begin("ple", (t, hf))
                product(out[0:rows, :], lambda c: p_t[:, c, tok:tok + rows], lambda c: w_ple[:, c, f], KP).then_inc(filled, 1)

            for n, (t, j) in enumerate(V_LIST):
                last_stage(n, {"h3T": turn_h3, "ple_0": lambda t: ple(t, 0), "ple_1": lambda t: ple(t, 1)})
                if by_vector(t, j):
                    continue
                if j == 0 and t >= 2:
                    pe.wait_ge(sem("x2_ready"), t - 1)
                k = V_ORDINAL[n]
                last = t < SAMPLE and j == max(i for i in range(GATHERS[t]) if not by_vector(t, i))
                pe.wait_ge(v_loaded[n % VSLOTS], 16 * (n // VSLOTS + 1))
                pe.wait_ge(sem("diag"), k + 1)
                m = P if t < SAMPLE else DEC
                for hf in range(2):
                    f = slice(hf * 512, (hf + 1) * 512)
                    ins = pe.matmul(acc[t % 2][0:m, f], diag[:, k % DIAGS, 0:m], vring[:, n % VSLOTS, f],
                                    start=(j == 0), stop=last)
                ins.then_inc(v_tensor, 1)
            pe.wait_ge(v_vector, len(V_VECTOR))
            for hf in range(2):
                f = slice(hf * 512, (hf + 1) * 512)
                ins = pe.matmul(acc[SAMPLE % 2][0:DEC, f], fold[:], side[:, f], start=False, stop=True)
            ins.then_inc(v_tensor, 1)
            turn_h3(SAMPLE)
            ple(SAMPLE, 0)
            ple(SAMPLE, 1)

        @block.scalar
        def _(sc):
            ch = Chain(sc, sem("scalar_step"))

            def col(base, n=0):
                return cols[:, base + n:base + n + 1]

            def root(t, ready, count, src, junk, name):
                rows = TILES[t][2]
                sc.wait_ge(sem(ready), count)
                ch.step(sc.activation(junk, src, ACT.Square, accum_out=stat[0:rows, 24 + t:25 + t]))
                ch.go(sc.activation(stat[0:rows, 32 + t:33 + t], stat[0:rows, 24 + t:25 + t], ACT.Sqrt, scale=1.0 / D,
                                    bias=eps[0:rows, 0:1]), name)

            def top_exps(t):
                rows = TILES[t][2]
                sc.wait_ge(sem("top_ready"), t + 1)
                ch.go(sc.activation(top[0:rows], top[0:rows], ACT.Exp), "top_exps")

            sc.wait_ge(loaded["const"], 16 * 8)
            sc.wait_ge(loaded["cache"], 16 * 3)
            sc.wait_ge(sem("filled_const"), 3)
            for g in range(2):
                n_tok, tiles, cw = WIDTH[g], GROUPS[g], CONVW[g]
                sc.wait_ge(loaded[f"xT{g}"], 16)
                if g:
                    full(sc, "query", (PASSES[0][-1][0], SEGS - 1))
                ch.step(sc.activation(merged[:, :, 0:n_tok], hT[:, :, 0:n_tok], ACT.Square), "x_squared")
                full(sc, "ms", g)
                ch.step(sc.activation(tmp[:, 0:n_tok], bank("ms", g)[:, 0:n_tok], ACT.Sqrt, bias=eps[:, 0:1]), "rms_x")
                for stage, t in inner_stages(g):
                    if stage == "z" and t >= KC:
                        n = t
                        full(sc, "z", (g, n))
                        src, b = bank("z", (g, n))[:, 0:n_tok], col(C_BIN, n)
                        if n < Q0:
                            if g:
                                sc.wait_ge(sem("glu"), KC)
                            ch.step(sc.activation(sig[:, n - KC, 0:n_tok], src, ACT.Sigmoid, bias=b), "scalar_z")
                        elif n < K0:
                            ch.step(sc.activation(qT[:, n - Q0, 0:n_tok], src, ACT.Identity, bias=b), "scalar_z")
                        elif n == K0:
                            if g:
                                ch.step(sc.activation(kT[:, KCOLS - DEC:KCOLS], src[:, 2 * P:n_tok], ACT.Identity, bias=b))
                            at = WINDOW + START[g]
                            ch.step(sc.activation(kT[:, at:at + 2 * P], src[:, 0:2 * P], ACT.Identity, bias=b), "scalar_z")
                        elif n == V0:
                            ch.step(sc.activation(vT[:, 0:n_tok], src, ACT.Identity, bias=b), "scalar_z")
                        else:
                            ch.step(sc.activation(gates[:, n - G0, 0:n_tok], src, ACT.Sigmoid, bias=b), "scalar_z")
                    if stage == "tap_diags":
                        for w in range(TAPS):
                            ch.go(sc.activation(tap_diag[w], ident[:], ACT.Copy, scale=col(C_WDW, t * TAPS + w)), "tap_diags")
                    if stage == "conv_drain":
                        full(sc, "conv", t)
                        ch.step(sc.activation(conv[:, t, 0:cw], bank("conv", t)[:, 0:cw], ACT.Identity, bias=col(C_BDW, t)),
                                "conv_tensor")
                    if stage == "square":
                        sc.wait_ge(sem("centred"), g + 1)
                        ch.step(sc.activation(convsq[:, :, 0:cw], conv[:, :, 0:cw], ACT.Square), "conv_squared")
                    if stage == "var":
                        full(sc, "var", g)
                        ch.step(sc.activation(rstd[:, 0:cw], bank("var", g)[:, 0:cw], ACT.Sqrt, bias=eps[:, 0:1]), "rms_conv")
                    if stage in ("s", "e", "p"):
                        _, at, rows = TILES[t]
                        lo, hi = (P if t == 0 else 0), (2 * P if t < SAMPLE else WINDOW + DEC)
                        S, sm = att_S[t % 2], small[0:rows, t % 2, :]
                    if stage == "s":
                        if t == GROUPS[1][0]:
                            sc.wait_ge(sem("experts"), 1)
                        for j in range(PAIRS):
                            full(sc, "score", (t, j))
                            src = bank("score", (t, j))[0:rows, :].rearrange("p (k s) -> p k s", k=KV)[:, :, lo:hi]
                            ch.go(sc.activation(S[0:rows, 2 * j:2 * j + 2, lo:hi], src, ACT.Copy, scale=HD ** -0.5), "scores")
                    if stage == "e":
                        sc.wait_ge(sem("score_max"), t + 1)
                        for h in range(H):
                            ch.go(sc.activation(S[0:rows, h, lo:hi], S[0:rows, h, lo:hi], ACT.Exp,
                                                bias=sm[:, h:h + 1], accum_out=sm[:, 16 + h:17 + h]))
                        ch.go(sc.activation(sm[:, 24:32], sm[:, 24:32], ACT.Exp), "exps")
                    if stage == "p":
                        for j in range(PAIRS):
                            full(sc, "probT", (t, j))
                            src = bank("probT", (t, j)).rearrange("p (b q) -> p b q", b=4)
                            if t < SAMPLE:
                                part = slice(lo // P, 4, 1 + lo // P)
                                to = PT[:, 4 * j:4 * j + 4, :]
                                ch.go(sc.activation(to[:, part, :], src[:, part, :], ACT.Copy), "probs_t")
                            else:
                                to = PT[:, 4 * j:4 * j + 4, 0:rows]
                                ch.go(sc.activation(to[:, 0::2, :], src[:, 0::2, 0:rows], ACT.Copy))
                                ch.go(sc.activation(to[0:DEC, 1::2, :], src[0:DEC, 1::2, 0:rows], ACT.Copy), "probs_t")
                        full(sc, "attT", t)
                        src = bank("attT", t).rearrange("p (j q) -> p j q", j=PAIRS)
                        ch.go(sc.activation(attT[:, :, at:at + rows], src[:, :, 0:rows], ACT.Copy), "att_t")
                sc.wait_ge(sem("conv_normed"), g + 1)
                for c in range(KC):
                    for s, (tok, n_seg, at) in enumerate(SEG[g]):
                        last = c == KC - 1 and s == len(SEG[g]) - 1
                        ch.step(sc.activation(cT[:, c, tok:tok + n_seg], conv[:, c, at - STATE:at - STATE + n_seg],
                                              ACT.Silu, bias=col(C_BCLN, c), scale=col(C_GCLN, c)),
                                "silu" if last else None)
                for n in range(KD):
                    full(sc, "mix", (g, n))
                    ch.step(sc.activation(hT[:, n, 0:n_tok], bank("mix", (g, n))[:, 0:n_tok], ACT.Copy), "delta_t")
                for t in tiles:
                    rows = TILES[t][2]
                    if t == GROUPS[1][0]:
                        top_exps(1)
                    root(t, "x1_ready", 2 * (t + 1), x1[0:rows, t, :], h2[0:rows, t, :], "rms_x1")
                for part in PASSES[g]:
                    for t in part:
                        _, at, rows = TILES[t]
                        for hf in range(2):
                            full(sc, "h2T", (t, hf))
                            src = bank("h2T", (t, hf)).rearrange("p (c q) -> p c q", c=4)
                            ch.step(sc.activation(merged[:, 4 * hf:4 * hf + 4, at:at + rows], src[:, :, 0:rows], ACT.Copy), "h2_t")
                    lo, hi = TILES[part[0]][1], TILES[part[-1]][1] + TILES[part[-1]][2]
                    for what, k in peer_order(part):
                        if what == "query":
                            full(sc, "query", (part[0], k))
                            ch.step(sc.activation(gates[:, k, lo:hi], bank("query", (part[0], k))[:, 0:hi - lo], ACT.Copy), "query_t")
                        else:
                            t, j = k
                            rows = TILES[t][2]
                            full(sc, "keyscore", (t, j))
                            ch.go(sc.activation(key_S[t][0:rows, 4 * j:4 * j + 4, :].rearrange("p a b -> p (a b)"),
                                                bank("keyscore", (t, j))[0:rows, :], ACT.Copy), "key_scores")
                if g == 0:
                    top_exps(0)
                if g == 1:
                    for s in range(2):
                        full(sc, "state", s)
                        ch.go(sc.activation(stash[:, s, :], bank("state", s)[0:STATE, :], ACT.Copy), "conv_state")

            def gelu_tanh(t):
                sc.wait_ge(sem("gelu_in"), t + 1)
                th = tanh[:, 0:GATHERS[t]]
                ch.go(sc.activation(th, th, ACT.Tanh, scale=GELU_K), "gelu_tanh")

            def copy_h3(t):
                rows = TILES[t][2]
                for hf in range(2):
                    full(sc, "h3T", (t, hf))
                    src = bank("h3T", (t, hf)).rearrange("p (c q) -> p c q", c=4)
                    ch.go(sc.activation(h3T[:, 4 * hf:4 * hf + 4, 0:rows], src[:, :, 0:rows], ACT.Copy), "h3_t")

            def sigmoid(t):
                rows = TILES[t][2]
                for hf in range(2):
                    full(sc, "ple_gate", (t, hf))
                    ch.go(sc.activation(pgate[0:rows, hf * 512:(hf + 1) * 512], bank("ple_gate", (t, hf))[0:rows, :],
                                        ACT.Sigmoid), "ple_gate")

            def root2(t):
                rows = TILES[t][2]
                sc.wait_ge(loaded["late"], 16 * 5)
                root(t, "x2_ready", t + 1, x1[0:rows, t, :], h3[0:rows, :], "rms_x2")

            def root3(t):
                rows = TILES[t][2]
                root(t, "x3_ready", t + 1, x1[0:rows, t, :], pgate[0:rows, :], "rms_x3")

            parts = {"root2": root2, "h3T_copy": copy_h3, "sigmoid": sigmoid, "root3": root3}
            gelu_tanh(0)
            sc.wait_ge(sem("key_scores"), 4 * len(TILES))
            for n, (t, j) in enumerate(V_LIST):
                for c, (_, exps, _) in CHOICE.items():
                    if n == exps:
                        top_exps(c)
                last_stage(n, parts)
                if n + GELU_AHEAD - 2 in FIRST[1:5]:
                    gelu_tanh(FIRST.index(n + GELU_AHEAD - 2))
                if j == 0:
                    sc.wait_ge(sem("act"), t + 1)
                if by_vector(t, j):
                    continue
                k = V_ORDINAL[n]
                if k >= DIAGS:
                    sc.wait_ge(v_tensor, k - DIAGS + 1)
                m = ident[:] if t < SAMPLE else fold[:]
                sc.activation(diag[:, k % DIAGS, 0:P if t < SAMPLE else DEC], m, ACT.Copy,
                              scale=dot[:, COLUMN[t] + j:COLUMN[t] + j + 1]).then_inc(sem("diag"), 1)
            for do in parts.values():
                do(SAMPLE)

        @block.vector
        def _(ve):
            ch = Chain(ve, sem("vector_step"))

            def col(base, n=0):
                return cols[:, base + n:base + n + 1]

            def normed(t, out, src, gain, rms, ready):
                rows = TILES[t][2]
                ve.wait_ge(sem(rms), t + 1)
                ch.step(ve.reciprocal(stat[0:rows, 40 + t:41 + t], stat[0:rows, 32 + t:33 + t]))
                ch.step(ve.scalar_tensor_tensor(out, src, stat[0:rows, 40 + t:41 + t], gain[0:rows, :], ALU.mult, ALU.mult), ready)

            for buf, value in ((over_d, 1.0 / D), (over_c, 1.0 / DC), (eps[:], EPS)):
                ve.memset(buf, value).then_inc(sem("filled_const"), 1)
            ch.step(ve.memset(glu[:, :, 0:STATE], 0.0))
            ve.wait_ge(loaded["const"], 16 * 8)
            ve.wait_ge(loaded["cache"], 16 * 3)

            def trunk(g):
                n_tok, tiles, cw = WIDTH[g], GROUPS[g], CONVW[g]
                if g:
                    for _ in choosing[0]:
                        pass
                    choice_end(0)
                    early_dots(DOTS["choice_end"])
                ve.wait_ge(sem("rms_x"), g + 1)
                ch.step(ve.reciprocal(rstd[:, 0:n_tok], tmp[:, 0:n_tok]))
                for c in range(KD):
                    ch.go(ve.scalar_tensor_tensor(hT[:, c, 0:n_tok], hT[:, c, 0:n_tok], col(C_GMIX, c), rstd[:, 0:n_tok],
                                                    ALU.mult, ALU.mult), "h_ready" if c == KD - 1 else None)
                ch.settle()
                if g:
                    ch.step(ve.tensor_copy(glu[:, :, 0:STATE], glu[:, :, 2 * P:2 * P + STATE]))
                    ch.step(ve.tensor_copy(glu[:, :, 2 * P + STATE:2 * P + 2 * STATE], past[:]))
                    early_dots(DOTS["h"])
                base, blocks = KC * TAPS * g, CONV_BLOCKS[g]
                for stage, t in inner_stages(g):
                    if stage == "glu":
                        c = t
                        full(ve, "z", (g, c))
                        ve.wait_ge(sem("scalar_z"), len(SCALAR_Z) * g + c + 1)
                        for s, (tok, n_seg, at) in enumerate(SEG[g]):
                            ch.step(ve.scalar_tensor_tensor(glu[:, c, at:at + n_seg], bank("z", (g, c))[:, tok:tok + n_seg],
                                                            col(C_BIN, c), sig[:, c, tok:tok + n_seg], ALU.add, ALU.mult),
                                    "glu" if s == len(SEG[g]) - 1 else None)
                    if stage == "vtok":
                        rows = TILES[t][2]
                        full(ve, "vtok", t)
                        src = bank("vtok", t)
                        if t >= 3:
                            ch.step(ve.tensor_copy(ktok[0:rows, t - 3, :], src[0:rows, P:2 * P]))
                        ch.step(ve.tensor_copy(vtok[0:rows, t if t < SAMPLE else 5, :], src[0:rows, 0:P]), "tokens_v")
                    if stage == "conv":
                        for w in range(*t):
                            for c in range(blocks):
                                src, out = glu[:, c, w:w + cw], conv[:, c, 0:cw]
                                tap = col(C_WDW, c * TAPS + w)
                                if w == 0:
                                    ve.tensor_scalar(out, src, tap, col(C_BDW, c), ALU.mult, ALU.add).then_inc(sem("conv"), 1)
                                else:
                                    ve.wait_ge(sem("conv"), base + blocks * (w - 1) + c + 1)
                                    ve.scalar_tensor_tensor(out, src, tap, out, ALU.mult, ALU.add).then_inc(sem("conv"), 1)
                    if stage in ("s", "e"):
                        rows = TILES[t][2]
                        lo, hi = (P if t == 0 else 0), (2 * P if t < SAMPLE else WINDOW + DEC)
                        S, sm = att_S[t % 2], small[0:rows, t % 2, :]
                    if stage == "s":
                        ve.wait_ge(sem("scores"), PAIRS * (t + 1))
                        for h in range(H):
                            ch.go(ve.scalar_tensor_tensor(S[0:rows, h, lo:hi], dist[0:rows, lo:hi], -SLOPES[h],
                                                          S[0:rows, h, lo:hi], ALU.mult, ALU.add))
                        ch.settle()
                        ch.step(ve.tensor_reduce(sm[:, 8:16], S[0:rows, :, lo:hi], AX, ALU.max))
                        ch.step(ve.tensor_tensor(sm[:, 8:16], sm[:, 8:16], sinks[0:rows, :], ALU.max))
                        ch.go(ve.tensor_tensor(sm[:, 24:32], sinks[0:rows, :], sm[:, 8:16], ALU.subtract))
                        ch.step(ve.tensor_scalar(sm[:, 0:8], sm[:, 8:16], -1.0, None, ALU.mult), "score_max")
                    if stage == "e":
                        ve.wait_ge(sem("exps"), t + 1)
                        ch.step(ve.tensor_tensor(sm[:, 16:24], sm[:, 16:24], sm[:, 24:32], ALU.add))
                        ch.step(ve.reciprocal(sm[:, 16:24], sm[:, 16:24]))
                        ch.step(ve.tensor_tensor(S[0:rows, :, lo:hi], S[0:rows, :, lo:hi],
                                                 sm[:, 16:24].unsqueeze(2).to_broadcast([rows, H, hi - lo]), ALU.mult), "probs")
                    if stage == "dots":
                        early_dots(t)
                    if stage == "mean":
                        ve.wait_ge(sem("conv"), base + blocks * TAPS)
                        full(ve, "mean", g)
                        for c in range(KC):
                            ch.go(ve.tensor_tensor(conv[:, c, 0:cw], conv[:, c, 0:cw], bank("mean", g)[:, 0:cw], ALU.subtract),
                                    "centred" if c == KC - 1 else None)
                    if stage == "norm":
                        ve.wait_ge(sem("rms_conv"), g + 1)
                        ch.step(ve.reciprocal(rstd[:, 0:cw], rstd[:, 0:cw]))
                        ch.step(ve.tensor_tensor(conv[:, :, 0:cw], conv[:, :, 0:cw],
                                                 rstd[:, 0:cw].unsqueeze(1).to_broadcast([P, KC, cw]), ALU.mult), "conv_normed")
                ve.wait_ge(sem("scalar_z"), len(SCALAR_Z) * (g + 1))
                for n in range(KD):
                    full(ve, "attn_out", (g, n))
                    ch.go(ve.scalar_tensor_tensor(merged[:, n, 0:n_tok], bank("conv_out", (g, n))[:, 0:n_tok], col(C_BCOUT, n),
                                                    gates[:, n, 0:n_tok], ALU.add, ALU.mult))
                    ch.step(ve.tensor_tensor(tmp[:, 0:n_tok], bank("attn_out", (g, n))[:, 0:n_tok],
                                             gates[:, KD + n, 0:n_tok], ALU.mult))
                    ch.step(ve.tensor_tensor(merged[:, n, 0:n_tok], merged[:, n, 0:n_tok], tmp[:, 0:n_tok], ALU.add), "merged")
                    if g:
                        early_dots(DOTS["merged"])
                        if n % 2:
                            next(choosing[1])
                for _ in range(4 * g):
                    next(choosing[1])
                    early_dots(DOTS["mix"])
                ve.wait_ge(loaded["x"], 32)
                for t in tiles:
                    rows = TILES[t][2]
                    for hf in range(2):
                        full(ve, "x1", (t, hf))
                        f = slice(hf * 512, (hf + 1) * 512)
                        ch.go(ve.tensor_tensor(x1[0:rows, t, f], bank("x1", (t, hf))[0:rows, :], x1[0:rows, t, f], ALU.add), "x1_ready")
                for t in tiles:
                    rows = TILES[t][2]
                    normed(t, h2[0:rows, t, :], x1[0:rows, t, :], g_ffn, "rms_x1", "h2_ready")

            def choice(t):
                rows = TILES[t][2]
                scores = key_S[t][0:rows]
                cand = PT[0:rows].rearrange("p a b -> p (a b)").rearrange("p (r k) -> p r k", r=HEADS)

                def top16(lists):
                    n = len(lists)
                    for values, vals, _ in lists:
                        ch.lag(lambda: ve.max(vals[:, 0:8], values), 1)
                    for values, vals, places in lists:
                        ch.lag(lambda: ve.max_index(places[:, 0:8], vals[:, 0:8], values), n)
                    for values, vals, _ in lists:
                        ch.lag(lambda: ve.match_replace(values, vals[:, 0:8], values, LOWEST), n)
                    for values, vals, _ in lists:
                        ch.lag(lambda: ve.max(vals[:, 8:16], values), n)
                    for values, vals, places in lists:
                        ch.lag(lambda: ve.max_index(places[:, 8:16], vals[:, 8:16], values), n)

                for m in range(0, SEGS, 4):
                    ve.wait_ge(sem("key_scores"), 4 * t + m // 4 + 1)
                    top16([(scores[:, i, :], best[0:rows, i, :], bestid[0:rows, i, :]) for i in range(m, m + 4)])
                    yield
                ch.settle()
                ch.go(ve.tensor_copy(bestidf[0:rows], bestid[0:rows]))
                b = best[0:rows].rearrange("p (r two) k -> p r two k", two=2)
                grid = [rows, HEADS, TOPK, TOPK]
                c4 = cand.rearrange("p r (i j) -> p r i j", i=TOPK)
                ch.step(ve.tensor_tensor(c4, b[:, :, 0, :].unsqueeze(3).to_broadcast(grid),
                                         b[:, :, 1, :].unsqueeze(2).to_broadcast(grid), ALU.add))
                yield
                for r in range(0, HEADS, 4):
                    top16([(cand[:, i, :], top[0:rows, i, :], pos[0:rows, i, :]) for i in range(r, r + 4)])
                    yield
                ch.settle()
                ch.go(ve.tensor_scalar(pos[0:rows, HEADS:2 * HEADS], pos[0:rows, 0:HEADS], 4, None, ALU.logical_shift_right))
                ch.go(ve.tensor_scalar(pos[0:rows, 2 * HEADS:], pos[0:rows, 0:HEADS], TOPK - 1, None, ALU.bitwise_and))
                ch.step(ve.tensor_copy(stat[0:rows, 8:16], top[0:rows, :, 0]))
                ch.go(ve.tensor_copy(posf[0:rows], pos[0:rows, HEADS:]))
                ch.step(ve.tensor_tensor(top[0:rows], top[0:rows], stat[0:rows, 8:16].unsqueeze(2).to_broadcast([rows, HEADS, TOPK]),
                                         ALU.subtract), "top_ready")
                bi = bestidf[0:rows].rearrange("p (r two) k -> p r two k", two=2)
                for side in range(2):
                    places = posf[0:rows, side * HEADS:(side + 1) * HEADS, :].rearrange("p r k -> p (r k)")
                    hot = cand.rearrange("p r (k i) -> p (r k) i", i=TOPK)
                    flat = [rows, PICKS, TOPK]
                    ch.step(ve.tensor_tensor(hot, places.unsqueeze(2).to_broadcast(flat),
                                             iota[0:rows].unsqueeze(1).to_broadcast(flat), ALU.is_equal))
                    yield
                    ch.step(ve.tensor_tensor(c4, c4, bi[:, :, side, :].unsqueeze(2).to_broadcast(grid), ALU.mult))
                    yield
                    ch.step(ve.tensor_reduce(chosen[0:rows, side, :], hot, AX, ALU.add))
                    if side == 0:
                        yield
                at = slice(COLUMN[t], COLUMN[t] + PICKS)
                ch.step(ve.scalar_tensor_tensor(expert[0:rows, at], chosen[0:rows, 0, :], float(KEYS),
                                                chosen[0:rows, 1, :], ALU.mult, ALU.add), "experts")

            def choice_end(t):
                rows = TILES[t][2]
                at = slice(COLUMN[t], COLUMN[t] + PICKS)
                ve.wait_ge(sem("top_exps"), t + 1)
                ch.step(ve.tensor_reduce(stat[0:rows, 16:24], top[0:rows], AX, ALU.add))
                ch.step(ve.reciprocal(stat[0:rows, 16:24], stat[0:rows, 16:24]))
                ch.step(ve.tensor_tensor(gate[0:rows, at].rearrange("p (r k) -> p r k", r=HEADS),
                                         top[0:rows], stat[0:rows, 16:24].unsqueeze(2).to_broadcast([rows, HEADS, TOPK]),
                                         ALU.mult), "expert_weights")

            u_next = [0]

            def dots(n):
                for u in range(u_next[0], u_next[0] + n):
                    t, j = U_LIST[u]
                    if u == FIRST[SAMPLE]:
                        ve.wait_ge(loaded["h2_fold"], 16)
                    ve.wait_ge(u_loaded[u % USLOTS], 16 * (u // USLOTS + 1))
                    row = uring[:, u % USLOTS, :]
                    ve.tensor_tensor_reduce(row, row, h2[:, t, :], 1.0, 0.0, ALU.mult, ALU.add,
                                            dot[:, COLUMN[t] + j:COLUMN[t] + j + 1]).then_inc(u_used, 1)
                u_next[0] += n

            def early_dots(n):
                dots(min(n, GATHERS[0] - u_next[0]))

            def gelu_in(t):
                at = slice(COLUMN[t], COLUMN[t] + GATHERS[t])
                ve.wait_ge(u_used, FIRST[t + 1])
                if t == SAMPLE:
                    ve.wait_ge(loaded["id_fold"], 32)
                d, th = dot[:, at], tanh[:, 0:GATHERS[t]]
                ch.step(ve.tensor_tensor(th, d, d, ALU.mult))
                ch.step(ve.tensor_scalar(th, th, GELU_C, 1.0, ALU.mult, ALU.add))
                ch.go(ve.scalar_tensor_tensor(gate[:, at], gate[:, at], 0.5, d, ALU.mult, ALU.mult))
                ch.step(ve.tensor_tensor(th, th, d, ALU.mult), "gelu_in")

            def gelu_out(t):
                at = slice(COLUMN[t], COLUMN[t] + GATHERS[t])
                ve.wait_ge(sem("gelu_tanh"), t + 1)
                ch.step(ve.scalar_tensor_tensor(dot[:, at], tanh[:, 0:GATHERS[t]], 1.0, gate[:, at], ALU.add, ALU.mult), "act")

            choosing = {t: choice(t) for t in range(len(TILES))}
            for g in range(2):
                trunk(g)
            for _ in choosing[1]:
                early_dots(DOTS["choice"])
            choice_end(1)
            dots(PHASE1 - u_next[0])
            gelu_in(0)
            gelu_out(0)

            def sum_up(t):
                rows = TILES[t][2]
                ve.wait_ge(v_tensor, len([n for n in V_TENSOR if n < FIRST[t + 1]]) + (t == SAMPLE))
                ve.wait_ge(v_vector, len([n for n in V_VECTOR if n < FIRST[t + 1]]))
                ch.step(ve.tensor_tensor(x1[0:rows, t, :], acc[t % 2][0:rows, :], x1[0:rows, t, :], ALU.add), "x2_ready")

            def h3_of(t):
                rows = TILES[t][2]
                normed(t, h3[0:rows, :], x1[0:rows, t, :], gains[:, 0, :], "rms_x2", "h3_ready")

            def x3_of(t):
                rows = TILES[t][2]
                for hf in range(2):
                    f = slice(hf * 512, (hf + 1) * 512)
                    ve.wait_ge(sem("ple_gate"), 2 * t + hf + 1)
                    full(ve, "ple", (t, hf))
                    ch.go(ve.tensor_tensor(pgate[0:rows, f], bank("ple", (t, hf))[0:rows, :], pgate[0:rows, f], ALU.mult), "x3_half")
                ch.settle()
                ch.step(ve.tensor_tensor(x1[0:rows, t, :], x1[0:rows, t, :], pgate[0:rows, :], ALU.add), "x3_ready")

            def y_of(t):
                rows = TILES[t][2]
                if t >= 2:
                    ve.wait_ge(sem(f"y_stored{t % 2}"), 16 * (t // 2))
                normed(t, y[0:rows, t % 2, :], x1[0:rows, t, :], gains[:, 1, :], "rms_x3", "y_ready")

            parts = {"sum": sum_up, "h3": h3_of, "x3": x3_of, "y": y_of}
            for n, (t, j) in enumerate(V_LIST):
                if n + GELU_AHEAD in FIRST[1:5]:
                    gelu_in(FIRST.index(n + GELU_AHEAD))
                if n + GELU_AHEAD - 4 in FIRST[1:5]:
                    gelu_out(FIRST.index(n + GELU_AHEAD - 4))
                for c, (begin, _, end) in CHOICE.items():
                    if begin <= n < end and (n - begin) % CHOICE_STRIDE == 0:
                        next(choosing[c], None)
                    if n == end:
                        choice_end(c)
                last_stage(n, parts)
                dots(U_BY[n] - u_next[0])
                if by_vector(t, j):
                    k = V_ORDINAL[n]
                    ve.wait_ge(v_loaded[n % VSLOTS], 16 * (n // VSLOTS + 1))
                    if k:
                        ve.wait_ge(v_vector, k)
                    row, scale = vring[:, n % VSLOTS, :], dot[:, COLUMN[t] + j:COLUMN[t] + j + 1]
                    if t < SAMPLE:
                        ve.scalar_tensor_tensor(x1[:, t, :], row, scale, x1[:, t, :], ALU.mult, ALU.add).then_inc(v_vector, 1)
                    elif n == V_VECTOR[SAMPLE_VECTOR]:
                        ve.tensor_scalar(side, row, scale, None, ALU.mult).then_inc(v_vector, 1)
                    else:
                        ve.scalar_tensor_tensor(side, row, scale, side, ALU.mult, ALU.add).then_inc(v_vector, 1)
            for do in parts.values():
                do(SAMPLE)

        @block.gpsimd
        def _(po):
            def gather_u(n):
                t, j = U_LIST[n]
                if j == 0:
                    po.wait_ge(sem("experts"), t + 1)
                    if t == SAMPLE:
                        po.wait_ge(loaded["id_fold"], 32)
                if n >= USLOTS:
                    po.wait_ge(u_used, n - USLOTS + 1)
                c = COLUMN[t] + j
                po.indirect_dma_start(uring[:, n % USLOTS, :], None, a["expert_u"],
                                      bass.IndirectOffsetOnAxis(ap=expert[:, c:c + 1], axis=0)).then_inc(u_loaded[n % USLOTS], 16)

            def gather_v(n):
                t, j = V_LIST[n]
                if n >= VSLOTS:
                    m = n - VSLOTS
                    po.wait_ge(v_vector if by_vector(*V_LIST[m]) else v_tensor, V_ORDINAL[m] + 1)
                c = COLUMN[t] + j
                po.indirect_dma_start(vring[:, n % VSLOTS, :], None, a["expert_v"],
                                      bass.IndirectOffsetOnAxis(ap=expert[:, c:c + 1], axis=0)).then_inc(v_loaded[n % VSLOTS], 16)

            for n in range(PHASE1):
                gather_u(n)
            po.wait_ge(sem("key_scores"), 4 * len(TILES))
            for n in range(BEATS):
                gather_v(n)
                for u in range(U_BY[n - 1] if n else PHASE1, U_BY[n]):
                    gather_u(u)


_OUTS = {"y_p": (SEQ, D), "y_s": (DEC, D), "nk_p": (WINDOW, KV * HD), "nv_p": (WINDOW, KV * HD), "nc_p": (STATE, DC),
         "nk_s": (WINDOW, KV * HD), "nv_s": (WINDOW, KV * HD), "nc_s": (STATE, DC)}


def _blocks(w, n, k):
    return np.ascontiguousarray(w.reshape(k, P, n, P).transpose(2, 1, 0, 3))


def _rows(w, k):
    return np.ascontiguousarray(w.reshape(k, P, -1).transpose(1, 0, 2))


def _column(v):
    return v.reshape(-1, P).T


def layout(i):
    i = {k: np.asarray(v) for k, v in i.items()}
    x = np.concatenate([i["x_prompt"][0], i["x_sample"][0]])
    pe = np.concatenate([i["p_prompt"][0, 0], i["p_sample"][0, 0]])
    heads = np.arange(H * HD).reshape(KV, PAIRS, HD).transpose(1, 0, 2).reshape(-1)
    order = np.arange(NZ * P)
    order[Q0 * P:K0 * P] = Q0 * P + heads
    w_in, b_in = i["w_in"][0][:, order], i["b_in"][0][order]
    w_br = np.concatenate([i["w_cout"][0], i["w_aout"][0][heads]])
    q, k = np.arange(P)[:, None], np.arange(2 * P)[None, :]
    first = q // CHUNK * CHUNK
    seen = (k >= first) & (k < first + WINDOW + CHUNK)
    dist = np.where(seen, np.abs(q + WINDOW - k), 1e32).astype(np.float32)
    cols = np.concatenate([
        _column(b_in), _column(i["g_mix"][0]), _column(i["b_dw"][0]), _column(i["g_cln"][0]), _column(i["b_cln"][0]),
        _column(i["b_cout"][0]), i["w_dw"][0].reshape(TAPS, KC, P).transpose(2, 1, 0).reshape(P, -1)], axis=1)
    keys = np.stack([i["sub_keys1"][0], i["sub_keys2"][0]])
    return {
        "x_t": _rows(x.T, KD), "x_p": i["x_prompt"][0], "x_s": i["x_sample"][0], "p_t": _rows(pe.T, KP),
        "cols": cols, "ident": np.eye(P, dtype=np.float32), "fold": np.tile(np.eye(DEC, dtype=np.float32), (2, 1)), "dist": dist,
        "iota": np.tile(np.arange(TOPK, dtype=np.float32), (P, 1)), "keys_t": keys.transpose(2, 0, 1),
        "sinks": i["sinks"], "g_ffn": i["g_ffn"], "g_ple": i["g_ple"], "g_final": i["g_final"][None],
        "cache_kt": i["cache_k"].reshape(WINDOW, P).T, "cache_k": i["cache_k"].reshape(WINDOW, P),
        "cache_v": i["cache_v"].reshape(WINDOW, P), "past_t": _rows(i["state_conv"][0, 0].T, KC),
        "w_in": _blocks(w_in, NZ, KD), "w_br": _blocks(w_br, KD, KD), "w_out": _blocks(i["w_out"][0], KD, KD),
        "w_query": _blocks(i["w_query"][0], SEGS, KD), "w_ple": _rows(i["w_ple"][0], KP), "w_pg": _rows(i["w_ple_gate"][0], KD),
        "expert_u": i["expert_u"][0], "expert_v": i["expert_v"][0],
    }


def kernel(**inputs):
    import concourse.bacc as bacc
    from concourse.bass_utils import run_bass_kernel_spmd

    arrays = {k: np.ascontiguousarray(v) for k, v in layout(inputs).items()}
    nc = bacc.Bacc("TRN2", target_bir_lowering=False, num_devices=1)
    a = {k: nc.dram_tensor(k, v.shape, F32, kind="ExternalInput").ap() for k, v in arrays.items()}
    a |= {k: nc.dram_tensor(k, s, F32, kind="ExternalOutput").ap() for k, s in _OUTS.items()}
    build(nc, a)
    r = run_bass_kernel_spmd(nc, [arrays], core_ids=[0]).results[0]
    kv = (1, 1, WINDOW, KV, HD)
    return (r["y_p"].reshape(1, SEQ, D), r["y_s"].reshape(1, DEC, D), r["nk_p"].reshape(kv), r["nv_p"].reshape(kv),
            r["nc_p"].reshape(1, 1, STATE, DC), r["nk_s"].reshape(kv), r["nv_s"].reshape(kv),
            r["nc_s"].reshape(1, 1, STATE, DC))
```
